# Optimizing a Trainium2 kernel written in Bass

```python
import jax, jax.numpy as jnp
from jax import lax
import numpy as np

D_MODEL = 1024
BATCH = 1
SEQ = 512
DEPTH = 1

CHUNK = 64
SG_BLOCK = 128
A_WIDTH = 1024
A_GROUPS = 8
A_GROUP_DIM = A_WIDTH // A_GROUPS
B_WIDTH = 1024
B_GROUPS = 8
CONV_WIDTH = 3
D_FF = 4 * D_MODEL
N_BRANCHES = 2
EPS = 1e-6
IN_COLS = 2 * A_WIDTH + 3 * B_WIDTH + N_BRANCHES * D_MODEL


def rmsnorm(x, g):
    xf = x.astype(jnp.float32)
    y = xf * lax.rsqrt(jnp.mean(xf * xf, axis=-1, keepdims=True) + EPS)
    return (y * g.astype(jnp.float32)).astype(x.dtype)

def chunk_mask():
    c = jnp.arange(SG_BLOCK) // CHUNK
    return c[None, :] <= c[:, None]

def spatial_gating(u, v, w_s, b_s):
    bsz, s, _ = v.shape
    vb = v.reshape(bsz, s // SG_BLOCK, SG_BLOCK, A_GROUPS, A_GROUP_DIM)
    w = jnp.where(chunk_mask()[None], w_s, jnp.zeros_like(w_s))
    mixed = jnp.einsum('gij,bnjgc->bnigc', w, vb) + b_s.T[None, None, :, :, None]
    return u * mixed.reshape(bsz, s, A_WIDTH)

def causal_dwconv(z, w):
    s = z.shape[1]
    zp = jnp.pad(z, ((0, 0), (CONV_WIDTH - 1, 0), (0, 0)))
    y = w[0] * zp[:, 0:s]
    for k in range(1, CONV_WIDTH):
        y = y + w[k] * zp[:, k:k + s]
    return y

def first_inputs(seed: int = 0) -> dict:
    key = jax.random.key(seed)
    ks = jax.random.split(key, 16)
    f32 = jnp.float32
    nrm = lambda k, shape, scale: jax.random.normal(k, shape, f32) * scale
    return {
        "x": nrm(ks[0], (BATCH, SEQ, D_MODEL), 1.0),
        "norm_mix_g": 1.0 + nrm(ks[1], (DEPTH, D_MODEL), 0.1),
        "w_in": nrm(ks[2], (DEPTH, D_MODEL, IN_COLS), D_MODEL ** -0.5),
        "b_gate": nrm(ks[3], (DEPTH, N_BRANCHES * D_MODEL), 0.01),
        "norm_v_g": 1.0 + nrm(ks[4], (DEPTH, A_WIDTH), 0.1),
        "w_s": nrm(ks[5], (DEPTH, A_GROUPS, SG_BLOCK, SG_BLOCK), SG_BLOCK ** -0.5),
        "b_s": 1.0 + nrm(ks[6], (DEPTH, A_GROUPS, SG_BLOCK), 0.1),
        "conv_w": nrm(ks[7], (DEPTH, CONV_WIDTH, B_WIDTH), CONV_WIDTH ** -0.5),
        "w_proj_a": nrm(ks[8], (DEPTH, A_WIDTH, D_MODEL), A_WIDTH ** -0.5),
        "w_proj_b": nrm(ks[9], (DEPTH, B_WIDTH, D_MODEL), B_WIDTH ** -0.5),
        "w_out": nrm(ks[10], (DEPTH, D_MODEL, D_MODEL), D_MODEL ** -0.5),
        "norm_ff_g": 1.0 + nrm(ks[11], (DEPTH, D_MODEL), 0.1),
        "w_ff1": nrm(ks[12], (DEPTH, D_MODEL, D_FF), D_MODEL ** -0.5),
        "w_ff2": nrm(ks[13], (DEPTH, D_FF, D_MODEL), D_FF ** -0.5),
        "norm_final_g": 1.0 + nrm(ks[14], (D_MODEL,), 0.1),
    }

def first_block(x, norm_mix_g, w_in, b_gate, norm_v_g, w_s, b_s, conv_w, w_proj_a, w_proj_b,
              w_out, norm_ff_g, w_ff1, w_ff2, norm_final_g):
    split_at = [A_WIDTH, 2 * A_WIDTH, 2 * A_WIDTH + B_WIDTH, 2 * A_WIDTH + 2 * B_WIDTH,
                2 * A_WIDTH + 3 * B_WIDTH, 2 * A_WIDTH + 3 * B_WIDTH + D_MODEL]
    for l in range(DEPTH):
        h = rmsnorm(x, norm_mix_g[l])
        proj = jnp.einsum('bsd,dc->bsc', h, w_in[l])
        u, v, bg, cg, xs, ga, gb = jnp.split(proj, split_at, axis=-1)
        ga = ga + b_gate[l, :D_MODEL]
        gb = gb + b_gate[l, D_MODEL:]

        u = jax.nn.gelu(u, approximate=False)
        v = rmsnorm(jax.nn.gelu(v, approximate=False), norm_v_g[l])
        a = spatial_gating(u, v, w_s[l], b_s[l])

        c = bg * causal_dwconv(cg * xs, conv_w[l])

        m = (jax.nn.sigmoid(ga) * jnp.einsum('bsc,cd->bsd', a, w_proj_a[l])
             + jax.nn.sigmoid(gb) * jnp.einsum('bsc,cd->bsd', c, w_proj_b[l]))
        x = x + jnp.einsum('bsd,de->bse', m, w_out[l])

        hf = rmsnorm(x, norm_ff_g[l])
        z = jax.nn.relu(jnp.einsum('bsd,df->bsf', hf, w_ff1[l]))
        x = x + jnp.einsum('bsf,fd->bsd', z * z, w_ff2[l])
    return rmsnorm(x, norm_final_g)


Q_BLOCK = 128
SB_HEAD_DIM = 64
SB_HEADS = (D_MODEL // 2) // SB_HEAD_DIM
SB_WIDTH = SB_HEADS * SB_HEAD_DIM
GLA_HEADS = 4
GLA_DV = (D_MODEL // 2) // GLA_HEADS
GLA_DK = GLA_DV // 2
GLA_VWIDTH = GLA_HEADS * GLA_DV
GLA_KWIDTH = GLA_HEADS * GLA_DK
GLA_GATE_RANK = 16
GLA_TAU = 16.0
MIX_WIDTH = SB_WIDTH + GLA_VWIDTH
D_FF_2 = 2816
N_MOD = 6
IN_SPLITS = (SB_WIDTH, SB_WIDTH, SB_WIDTH,
             GLA_KWIDTH, GLA_KWIDTH, GLA_VWIDTH,
             GLA_VWIDTH, GLA_GATE_RANK)
IN_WIDTH = sum(IN_SPLITS)


def rms_norm(x, gain):
    xf = x.astype(jnp.float32)
    n = xf * lax.rsqrt(jnp.mean(xf * xf, axis=-1, keepdims=True) + EPS)
    return (n * gain.astype(jnp.float32)).astype(x.dtype)

def modulate(h, shift, scale):
    return h * (1 + scale[:, None, :]) + shift[:, None, :]

def stick_breaking_attention(q, k, v):
    B, S, H, d = q.shape
    q = q.transpose(0, 2, 1, 3)
    k = k.transpose(0, 2, 1, 3)
    v = v.transpose(0, 2, 1, 3)
    scale = d ** -0.5
    outs = []
    for i in range(S // Q_BLOCK):
        start = i * Q_BLOCK
        end = start + Q_BLOCK
        qb = q[:, :, start:end]
        kb = k[:, :, :end]
        vb = v[:, :, :end]
        z = jnp.einsum('bhqd,bhkd->bhqk', qb, kb).astype(jnp.float32) * scale
        t_pos = start + jnp.arange(Q_BLOCK)
        s_pos = jnp.arange(end)
        mask = s_pos[None, :] < t_pos[:, None]
        log_one_minus = jnp.where(mask, jax.nn.log_sigmoid(-z), 0.0)
        shifted = jnp.concatenate(
            [log_one_minus[..., 1:], jnp.zeros_like(log_one_minus[..., :1])], axis=-1)
        between = lax.cumsum(shifted, axis=3, reverse=True)
        weights = jnp.where(mask, jnp.exp(jax.nn.log_sigmoid(z) + between), 0.0)
        outs.append(jnp.einsum('bhqk,bhkd->bhqd', weights.astype(vb.dtype), vb))
    o = jnp.concatenate(outs, axis=2)
    return o.transpose(0, 2, 1, 3).reshape(B, S, H * d)

def gla_chunk_causal(q, k, v, log_alpha):
    B, S, H, dk = q.shape
    dv = v.shape[-1]
    nc = S // CHUNK
    qc = q.reshape(B, nc, CHUNK, H, dk).astype(jnp.float32) * (dk ** -0.5)
    kc = k.reshape(B, nc, CHUNK, H, dk).astype(jnp.float32)
    vc = v.reshape(B, nc, CHUNK, H, dv).astype(jnp.float32)
    la = log_alpha.reshape(B, nc, CHUNK, H, dk).astype(jnp.float32)
    cum = jnp.cumsum(la, axis=2)
    total = cum[:, :, -1]
    k_dec = kc * jnp.exp(total[:, :, None] - cum)
    chunk_kv = jnp.einsum('bnchk,bnchv->nbhkv', k_dec, vc)
    chunk_decay = jnp.exp(total).transpose(1, 0, 2, 3)

    def step(state, inp):
        decay, kv = inp
        state = decay[..., None] * state + kv
        return state, state

    s0 = jnp.zeros((B, H, dk, dv), jnp.float32)
    _, states = lax.scan(step, s0, (chunk_decay, chunk_kv))
    o = jnp.einsum('bnchk,nbhkv->bnchv', qc, states)
    return o.reshape(B, S, H * dv)

def causal_depthwise_conv(u, w, b):
    S = u.shape[1]
    up = jnp.pad(u, ((0, 0), (CONV_WIDTH - 1, 0), (0, 0)))
    out = b
    for j in range(CONV_WIDTH):
        out = out + w[j] * up[:, j:j + S]
    return out

def second_inputs(seed: int = 0) -> dict:
    key = jax.random.key(seed)
    ks = jax.random.split(key, 18)

    def nrm(k, shape, scale):
        return jax.random.normal(k, shape, jnp.float32) * scale

    L, D = DEPTH, D_MODEL
    return {
        "x": nrm(ks[0], (BATCH, SEQ, D), 1.0),
        "c": nrm(ks[1], (BATCH, D), 1.0),
        "w_ada": nrm(ks[2], (L, D, N_MOD * D), 0.5 * D ** -0.5),
        "b_ada": nrm(ks[3], (L, N_MOD * D), 0.01),
        "g_norm1": 1.0 + nrm(ks[4], (L, D), 0.02),
        "w_in": nrm(ks[5], (L, D, IN_WIDTH), D ** -0.5),
        "w_fg2": nrm(ks[6], (L, GLA_GATE_RANK, GLA_KWIDTH), GLA_GATE_RANK ** -0.5),
        "b_fg2": nrm(ks[7], (L, GLA_KWIDTH), 0.1),
        "g_gla_out": 1.0 + nrm(ks[8], (L, GLA_VWIDTH), 0.02),
        "w_out": nrm(ks[9], (L, MIX_WIDTH, D), MIX_WIDTH ** -0.5),
        "g_norm2": 1.0 + nrm(ks[10], (L, D), 0.02),
        "w_up": nrm(ks[11], (L, D, 2 * D_FF_2), D ** -0.5),
        "w_conv": nrm(ks[12], (L, CONV_WIDTH, 2 * D_FF_2), CONV_WIDTH ** -0.5),
        "b_conv": nrm(ks[13], (L, 2 * D_FF_2), 0.01),
        "w_down": nrm(ks[14], (L, D_FF_2, D), D_FF_2 ** -0.5),
        "g_final": 1.0 + nrm(ks[15], (D,), 0.02),
    }

def second_block(x, c, w_ada, b_ada, g_norm1, w_in, w_fg2, b_fg2, g_gla_out, w_out,
              g_norm2, w_up, w_conv, b_conv, w_down, g_final):
    B, S, _ = x.shape
    offsets = np.cumsum(IN_SPLITS)[:-1].tolist()
    for l in range(DEPTH):
        mod = jax.nn.silu(c) @ w_ada[l] + b_ada[l]
        shift1, scale1, gate1, shift2, scale2, gate2 = jnp.split(mod, N_MOD, axis=-1)

        h = modulate(rms_norm(x, g_norm1[l]), shift1, scale1)
        proj = h @ w_in[l]
        sb_q, sb_k, sb_v, gq, gk, gv, gg, gf = jnp.split(proj, offsets, axis=-1)

        o_sb = stick_breaking_attention(
            sb_q.reshape(B, S, SB_HEADS, SB_HEAD_DIM),
            sb_k.reshape(B, S, SB_HEADS, SB_HEAD_DIM),
            sb_v.reshape(B, S, SB_HEADS, SB_HEAD_DIM))

        log_alpha = jax.nn.log_sigmoid(
            (gf @ w_fg2[l] + b_fg2[l]).astype(jnp.float32)) / GLA_TAU
        o_gla = gla_chunk_causal(
            gq.reshape(B, S, GLA_HEADS, GLA_DK),
            gk.reshape(B, S, GLA_HEADS, GLA_DK),
            gv.reshape(B, S, GLA_HEADS, GLA_DV),
            log_alpha.reshape(B, S, GLA_HEADS, GLA_DK))
        oh = o_gla.reshape(B, S, GLA_HEADS, GLA_DV)
        oh = oh * lax.rsqrt(jnp.mean(oh * oh, axis=-1, keepdims=True) + EPS)
        o_gla = (oh.reshape(B, S, GLA_VWIDTH) * g_gla_out[l].astype(jnp.float32)
                 ).astype(x.dtype) * jax.nn.silu(gg)

        mixed = jnp.concatenate([o_sb.astype(x.dtype), o_gla], axis=-1) @ w_out[l]
        x = x + (1 + gate1[:, None, :]) * mixed

        h2 = modulate(rms_norm(x, g_norm2[l]), shift2, scale2)
        u = causal_depthwise_conv(h2 @ w_up[l], w_conv[l], b_conv[l])
        val, gte = jnp.split(u, 2, axis=-1)
        x = x + (1 + gate2[:, None, :]) * ((val * jax.nn.silu(gte)) @ w_down[l])
    return rms_norm(x, g_final)


def setup_inputs(seed=0):
    out = dict(first_inputs(seed))
    for name, value in second_inputs(seed + 1).items():
        if name != "x":
            out[name + "_2"] = value
    return out


def reference(
    x, norm_mix_g, w_in, b_gate, norm_v_g, w_s, b_s, conv_w, w_proj_a, w_proj_b, w_out,
    norm_ff_g, w_ff1, w_ff2, norm_final_g, c_2, w_ada_2, b_ada_2, g_norm1_2, w_in_2, w_fg2_2,
    b_fg2_2, g_gla_out_2, w_out_2, g_norm2_2, w_up_2, w_conv_2, b_conv_2, w_down_2, g_final_2,
):
    x = first_block(
        x, norm_mix_g, w_in, b_gate, norm_v_g, w_s, b_s, conv_w, w_proj_a, w_proj_b, w_out,
        norm_ff_g, w_ff1, w_ff2, norm_final_g,
    )
    return second_block(
        x, c_2, w_ada_2, b_ada_2, g_norm1_2, w_in_2, w_fg2_2, b_fg2_2, g_gla_out_2, w_out_2,
        g_norm2_2, w_up_2, w_conv_2, b_conv_2, w_down_2, g_final_2,
    )


_drawn_inputs = setup_inputs


def setup_inputs(seed=0):
    import zlib

    import numpy as np

    out = dict(_drawn_inputs(seed))
    spreads = {}
    factors = {'b_gate': 8.0,
     'g_norm1_2': 2.686,
     'g_gla_out_2': 6.492,
     'g_norm2_2': 3.897,
     'b_conv_2': 8.0,
     'g_final_2': 2.878}
    for name, (base, spread) in spreads.items():
        noise = np.random.default_rng([zlib.crc32(name.encode()), seed]).standard_normal(out[name].shape)
        drawn = base * np.exp(spread * noise) if base else spread * noise
        out[name] = __import__('jax').numpy.asarray(drawn.astype(out[name].dtype))
    for name, factor in factors.items():
        out[name] = (out[name] * factor).astype(out[name].dtype)
    return out
```

```python
from contextlib import ExitStack

import concourse.bass as bass
from concourse import mybir

P = 128
S = 512
D = 1024
KT = D // P
UNIT = 256
NBLK = S // P
EPS = 1e-6
F2 = 2816
SB_HEADS, SB_DIM = 8, 64
GLA_HEADS, DK, DV, CHUNK = 4, 64, 128, 64
NCH = S // CHUNK
RANK = 16
TAU = 16.0
NMOD = 6

F32 = mybir.dt.float32
F32R = mybir.dt.float32r
BF16 = mybir.dt.bfloat16
ALU = mybir.AluOpType
ACT = mybir.ActivationFunctionType

QUADS = [("v", 2), ("u", 2), ("ga", 2), ("pa", 2), ("cg", 2), ("xs", 2), ("bg", 2), ("gb", 2), ("pb", 2),
         ("out", 2), ("ff", 16), ("w2", 6), ("out2", 2), ("mlp", 12), ("last_up", 3), ("last_down", 2)]
FIRST = {}
for _name, _n in QUADS:
    FIRST[_name] = sum(n for _, n in QUADS[:len(FIRST)])
NQ = sum(n for _, n in QUADS)

OPERANDS = [("n1", 8), ("u", 8), ("bg", 8), ("pb", 8), ("n2", 8), ("ff", 32), ("n3", 8), ("gla", 4),
            ("n4", 8), ("mlp", 16), ("last", 6)]
MADE = {}
for _name, _n in OPERANDS:
    MADE[_name] = sum(n for _, n in OPERANDS[:len(MADE)])

VALUES = [(name, n) for name, n in OPERANDS if name != "bg"] + [("final", 8)]
VALUED = {}
for _name, _n in VALUES:
    VALUED[_name] = sum(n for _, n in VALUES[:len(VALUED)])

C_NMIX, C_BGATE, C_NV, C_CONV, C_NFF, C_C, C_NFIN = 0, 8, 24, 32, 56, 64, 72
C_BADA, C_G1, C_BFG, C_GGLA, C_G2, C_GFIN = 128, 176, 184, 186, 190, 198
C_WCONV, C_BCONV = 256, 388
F2T = 2 * F2 // P


ADA = 3 * P
N_ITEMS = 4 * SB_HEADS


def mixer_schedule():
    order = [("tile", 0)]
    for t in range(1, 4):
        order += [("tile", t), ("turn_v", t - 1)]
    order += [("tile", 4), ("turn_v", 3)] + [("tile", t) for t in range(5, 12)]
    step = 0

    def attend(n):
        nonlocal step
        for _ in range(n):
            if step < N_ITEMS:
                order.append(("z", step))
            if 1 <= step <= N_ITEMS:
                order.append(("tri", step - 1))
            if 2 <= step <= N_ITEMS + 1:
                order.append(("pv", step - 2))
            step += 1

    order += [("fg", 0), ("tile", 12), ("fg", 1), ("tile", 13), ("fg", 2)]
    for t, n, after in [(14, 2, []), (15, 2, []), (16, 2, [("turn_k", 0)]),
                        (17, 2, [("turn_k", 1), ("turn_gv", 0)]), (18, 2, [("turn_gv", 1)]),
                        (19, 2, [("turn_gv", 2)]), (20, 2, [("turn_gv", 3)]), (21, 2, []), (22, 2, []),
                        (23, 1, [])]:
        order += [("tile", t)] + after
        attend(n)
    for r in range(4):
        order.append(("kv", r))
        attend(1)
    for h in range(GLA_HEADS):
        order.append(("o", h))
        attend(1)
        order.append(("ms", h))
        attend(1)
    attend(N_ITEMS + 2 - step)
    return order


MIXER = mixer_schedule()
AUX2 = {e: n for n, e in enumerate(e for e in MIXER if e[0] in ("turn_v", "fg", "turn_k", "turn_gv", "kv", "o", "ms"))}


def item(m):
    h, i = m // 4, 3 - m % 4
    return h, i, P * i, S - P * i


def build(nc, a, out):
    ctx = ExitStack()
    with ctx:
        def sb(name, cols, dt=F32, parts=P):
            return ctx.enter_context(nc.sbuf_tensor(name, [parts, cols], dt))

        def sem(name):
            return ctx.enter_context(nc.semaphore(name))

        scratch = ExitStack()
        under_hi0 = scratch.enter_context(nc.sbuf_tensor("under_hi0", [P, KT * S], F32))
        under_lo0 = scratch.enter_context(nc.sbuf_tensor("under_lo0", [P, KT * S], F32))
        states = scratch.enter_context(nc.sbuf_tensor("states", [P, KT * S], F32))
        scratch.close()
        hi0 = sb("operand_hi0", KT * S, F32R)
        lo0 = sb("operand_lo0", KT * S, F32R)
        hi1 = sb("operand_hi1", KT * S, F32R)
        lo1 = sb("operand_lo1", KT * S, F32R)
        OP = [(hi0, lo0), (hi1, lo1)]
        raw = [sb(f"raw{j}", KT * UNIT) for j in range(2)]
        w_hi = [sb(f"weights_hi{k}", KT * P, F32R) for k in range(4)]
        w_lo = [sb(f"weights_lo{k}", KT * P, F32R) for k in range(4)]
        x = sb("x_features", KT * S)
        gates = sb("gates", KT * S)
        kept = sb("kept", KT * S)
        mixw = sb("mix_weights", 8 * P)
        mixb = sb("mix_bias", 8 * P)
        table = sb("vector_table", 512)
        mod = sb("modulation", NMOD * KT)
        scales = sb("mod_scales", 4 * KT)
        cvec = sb("c_silu", KT)
        ssum = sb("square_sums", S)
        rinv = sb("inverse_rms", S)
        tA = [sb(f"value{j}", S) for j in range(2)]
        tB = sb("evacuated", 2 * S)
        yb = sb("conv_or_gate", 4 * S)
        shared = sb("ada_or_attention", 6 * S)
        acc = sb("ada_sums", ADA)
        stat = sb("v_stats", 3 * NBLK)
        decay = sb("decay", 2 * NCH)
        raw_gf = sb("raw_gf", KT * RANK)
        ident = sb("identity", P)
        mean_d = sb("mean_of_width", P)
        mean_h = sb("mean_of_head", P)
        neg_one = sb("minus_ones", P)
        neg_tri = sb("minus_lower_triangle", P)
        before = sb("key_before_query", P)
        one = sb("one", 1)
        epsc = sb("eps", 1)

        ps = [ctx.enter_context(nc.psum_tensor(f"bank{k}", [P, S], F32)) for k in range(4)]
        aux = [ctx.enter_context(nc.psum_tensor(f"aux{k}", [P, S], F32)) for k in range(4)]

        gq = [mixw[:, p * S:(p + 1) * S] for p in range(2)]
        gk = [mixb[:, p * S:(p + 1) * S] for p in range(2)]
        gate_y = [under_hi0[:, (4 + p) * S:(5 + p) * S] for p in range(2)]
        gate_e = [under_hi0[:, (6 + p) * S:(7 + p) * S] for p in range(2)]
        k_tok = under_lo0[:, 4 * S:6 * S]
        gf_t = under_lo0[0:RANK, 6 * S:7 * S]
        wfg = yb[0:RANK, 0:2 * P]
        E = [shared[:, j * S:(j + 1) * S] for j in range(3)]
        SP = [shared[:, (3 + j) * S:(4 + j) * S] for j in range(2)]
        later = shared[:, 5 * S:6 * S]
        ada_raw = shared[:, 0:KT * ADA]
        v_tok = kept[:, 0:4 * S]
        gv_tok = kept[:, 4 * S:8 * S]
        vec_rows = kept[:, 0:512]
        ws_rows = kept[:, 1024:2048]

        def tb(j):
            return tB[:, j * S:(j + 1) * S]

        def tile(buf, n):
            return buf[:, bass.ds(n * S, S)]

        def col(c, n=1):
            return table[:, bass.ds(c, n)]

        vec_loaded, ws_loaded, x_loaded, small_loaded = (sem(n) for n in ("vec_loaded", "ws_loaded", "x_loaded", "small_loaded"))
        consts, masks_begun = sem("consts"), sem("masks_begun")
        rows_turned, table_kept, ws_turned, ws_kept, x_turned, x_kept = (
            sem(n) for n in ("rows_turned", "table_kept", "ws_turned", "ws_kept", "x_turned", "x_kept"))
        c_ready = sem("c_ready")
        raw_landed = [sem(f"raw_landed{j}") for j in range(2)]
        w_hi_done, w_lo_done, tile_done = sem("w_hi_done"), sem("w_lo_done"), sem("tile_done")
        bank_read = [sem(f"bank_read{k}") for k in range(4)]
        value, act_hi, operand = sem("value"), sem("act_hi"), sem("operand")
        sq_done, sum_added, norm_summed, rms_done, inv_done = (
            sem(n) for n in ("sq_done", "sum_added", "norm_summed", "rms_done", "inv_done"))
        v_turned, v_kept, v_sumsq, v_rms, v_inv, v_normed = (
            sem(n) for n in ("v_turned", "v_kept", "v_sumsq", "v_rms", "v_inv", "v_normed"))
        mixed, mix_biased, tap0, tap1, tap2 = (sem(n) for n in ("mixed", "mix_biased", "tap0", "tap1", "tap2"))
        ada_landed, ada_step, ada_turned, mod_done = (sem(n) for n in ("ada_landed", "ada_step", "ada_turned", "mod_done"))
        silu_done = sem("silu_done")
        aux2_filled, aux2_read = sem("aux2_filled"), sem("aux2_read")
        gf_zeroed, gf_hi, gf_lo = sem("gf_zeroed"), sem("gf_hi"), sem("gf_lo")
        g_abs, g_exp, g_log, g_sp, g_cum, g_rest, g_dec, k_dec, g_state, o_sq, g_inv, g_scaled = (
            sem(n) for n in ("g_abs", "g_exp", "g_log", "g_sp", "g_cum", "g_rest", "g_dec", "k_dec", "g_state",
                             "o_sq", "g_inv", "g_scaled"))
        reset_ready = sem("reset_ready")
        z_done, z_abs, z_exp, z_log, sp_raw, sp_done, tri_done, w_exp, w_masked, pv_done, later_done = (
            sem(n) for n in ("z_done", "z_abs", "z_exp", "z_log", "sp_raw", "sp_done", "tri_done", "w_exp",
                             "w_masked", "pv_done", "later_done"))
        attn_hi, attn_lo = sem("attn_hi"), sem("attn_lo")
        out_turned, out_kept, out_written = sem("out_turned"), sem("out_kept"), sem("out_written")

        block = ctx.enter_context(nc.Block())

        F = FIRST
        MIX_Q = F["w2"]
        LAST_K = (F2 - 2 * D) // P
        mixer_columns = [2 * S, 2 * S + UNIT, 0, UNIT, S, S + UNIT, 3 * S, 3 * S + UNIT,
                         4 * S, 4 * S + UNIT, 5 * S, 5 * S + UNIT]
        NORM = {name: n for n, name in enumerate(["n1", "n2", "between", "n3", "n4", "final"])}

        def rows(w):
            return w.rearrange("(k p) n -> p k n", p=P)

        @block.sync
        def _(sp):
            xt = a["x"][0].rearrange("(b p) n -> p b n", p=P)
            sp.dma_start(gates[:, :].rearrange("p (b n) -> p b n", b=NBLK), xt).then_inc(x_loaded, 16)

            def unit(q, j, w, row_tile, column, k_tiles=KT):
                if not (isinstance(q, int) and q == 0):
                    sp.wait_ge(w_lo_done, 4 * (q - 1) + 2 * j + 2)
                sp.dma_start(raw[j][:, 0:k_tiles * UNIT].rearrange("p (k n) -> p k n", n=UNIT),
                             rows(w)[:, bass.ds(row_tile, k_tiles), bass.ds(column, UNIT)])\
                  .then_inc(raw_landed[j], 16)

            def columns(q0, w, c0, n=2):
                with sp.Fori(0, n) as i:
                    for j in range(2):
                        unit(q0 + i, j, w, 0, c0 + 2 * UNIT * i + UNIT * j)

            w_in = a["w_in"][0]
            for j in range(2):
                unit(0, j, w_in, 0, D + UNIT * j)
            for j in range(2):
                unit(1, j, w_in, 0, D + 2 * UNIT + UNIT * j)
            columns(F["u"], w_in, 0)
            columns(F["ga"], w_in, 5 * D)
            columns(F["pa"], a["w_proj_a"][0], 0)
            columns(F["cg"], w_in, 3 * D)
            columns(F["xs"], w_in, 4 * D)
            columns(F["bg"], w_in, 2 * D)
            columns(F["gb"], w_in, 6 * D)
            columns(F["pb"], a["w_proj_b"][0], 0)
            columns(F["out"], a["w_out"][0], 0)
            with sp.Fori(0, 4) as c:
                for part in range(2):
                    with sp.Fori(0, 2) as i:
                        q = F["ff"] + 4 * c + 2 * part + i
                        piece = 4 * c + 2 * part + i
                        for j in range(2):
                            if part == 0:
                                unit(q, j, a["w_ff1"][0], 0, D * c + 2 * UNIT * i + UNIT * j)
                            else:
                                unit(q, j, a["w_ff2"][0], KT * c, 2 * UNIT * i + UNIT * j)
                        sp.wait_ge(ada_step, 1 + KT * piece)
                        sp.dma_start(ada_raw.rearrange("p (k n) -> p k n", n=ADA),
                                     rows(a["w_ada_2"][0])[:, :, bass.ds(ADA * piece, ADA)])\
                          .then_inc(ada_landed, 16)
            for u, c0 in enumerate(mixer_columns):
                unit(MIX_Q + u // 2, u % 2, a["w_in_2"][0], 0, c0)
            columns(F["out2"], a["w_out_2"][0], 0)
            w_up, w_down = a["w_up_2"][0], a["w_down_2"][0]
            with sp.Fori(0, 2) as c:
                with sp.Fori(0, 4) as i:
                    for j in range(2):
                        unit(F["mlp"] + 6 * c + i, j, w_up, 0, D * c + UNIT * i + F2 * j)
                with sp.Fori(0, 2) as i:
                    for j in range(2):
                        unit(F["mlp"] + 6 * c + 4 + i, j, w_down, KT * c, 2 * UNIT * i + UNIT * j)
            for i in range(3):
                for j in range(2):
                    unit(F["last_up"] + i, j, w_up, 0, 2 * D + UNIT * i + F2 * j)
            for i in range(2):
                for j in range(2):
                    unit(F["last_down"] + i, j, w_down, 2 * KT, 2 * UNIT * i + UNIT * j, LAST_K)

            ov = out[0].rearrange("(b p) n -> p b n", p=P)
            gv = gates[:, :].rearrange("p (b n) -> p b n", b=NBLK)
            for half in range(2):
                sp.wait_ge(out_kept, 4 * (half + 1))
                sp.dma_start(ov[:, :, half * S:(half + 1) * S], gv[:, :, half * S:(half + 1) * S])\
                  .then_inc(out_written, 16)
            sp.wait_ge(out_written, 32)

        @block.gpsimd
        def _(pool):
            vec = vec_rows.rearrange("p (g c) -> p g c", g=4)

            def load_rows(group, row, v, n):
                pool.dma_start(vec[row:row + n, group, :], v.rearrange("(r c) -> r c", c=P)).then_inc(vec_loaded, 16)

            load_rows(0, 0, a["norm_mix_g"][0], 8)
            load_rows(0, 8, a["b_gate"][0], 16)
            load_rows(0, 24, a["norm_v_g"][0], 8)
            load_rows(0, 32, a["conv_w"][0].rearrange("k n -> (k n)"), 24)
            load_rows(0, 56, a["norm_ff_g"][0], 8)
            load_rows(0, 64, a["c_2"][0], 8)
            load_rows(0, 72, a["norm_final_g"], 8)
            load_rows(1, 0, a["b_ada_2"][0], 48)
            load_rows(1, 48, a["g_norm1_2"][0], 8)
            load_rows(1, 56, a["b_fg2_2"][0], 2)
            load_rows(1, 58, a["g_gla_out_2"][0], 4)
            load_rows(1, 62, a["g_norm2_2"][0], 8)
            load_rows(1, 70, a["g_final_2"], 8)
            w_conv = a["w_conv_2"][0].rearrange("k n -> (k n)")
            load_rows(2, 0, w_conv[0:P * P], P)
            load_rows(3, 0, w_conv[P * P:], 3 * F2T - P)
            load_rows(3, 3 * F2T - P, a["b_conv_2"][0], F2T)
            pool.dma_start(ws_rows.rearrange("p (g j) -> p g j", g=8),
                           a["w_s"][0].rearrange("g i j -> i g j")).then_inc(ws_loaded, 16)
            pool.dma_start(mixb[:, :], a["b_s"][0].rearrange("g i -> (g i)").partition_broadcast(P)).then_inc(small_loaded, 16)
            pool.dma_start(wfg, a["w_fg2_2"][0]).then_inc(small_loaded, 16)
            pool.dma_start(raw_gf[:, :].rearrange("p (k n) -> p k n", n=RANK),
                           rows(a["w_in_2"][0])[:, :, 6 * S:6 * S + RANK]).then_inc(small_loaded, 16)

            pool.memset(ident[:, :], 0.0).then_inc(masks_begun, 1)
            pool.memset(neg_tri[:, :], -1.0).then_inc(masks_begun, 1)
            pool.memset(before[:, :], 1.0).then_inc(masks_begun, 1)
            pool.wait_ge(masks_begun, 3)
            pool.affine_select(out=ident[:, :], in_=ident[:, :], compare_op=ALU.not_equal, fill=1.0, base=0,
                               pattern=[[-1, P]], channel_multiplier=1).then_inc(consts, 1)
            pool.affine_select(out=neg_tri[:, :], in_=neg_tri[:, :], compare_op=ALU.is_ge, fill=0.0, base=0,
                               pattern=[[-1, P]], channel_multiplier=1).then_inc(consts, 1)
            pool.affine_select(out=before[:, :], in_=before[:, :], compare_op=ALU.is_gt, fill=0.0, base=0,
                               pattern=[[1, P]], channel_multiplier=-1).then_inc(consts, 1)
            pool.memset(mean_d[:, :], 1.0 / D).then_inc(consts, 1)
            pool.memset(mean_h[:, :], 1.0 / DV).then_inc(consts, 1)
            pool.memset(neg_one[:, :], -1.0).then_inc(consts, 1)
            pool.memset(one[:, :], 1.0).then_inc(consts, 1)
            pool.memset(epsc[:, :], EPS).then_inc(consts, 1)

            for m in range(N_ITEMS):
                pool.wait_ge(w_exp, m + 1)
                e = E[m % 3][:, 0:P]
                pool.affine_select(out=e, in_=e, compare_op=ALU.is_gt, fill=0.0, base=0,
                                   pattern=[[1, P]], channel_multiplier=-1).then_inc(w_masked, 1)

        @block.tensor
        def _(pe):
            def stream_tile(q, k, op, ready, k_tiles=KT):
                pe.wait_ge(w_lo_done, 4 * q + k + 1)
                if not (isinstance(q, int) and q == 0):
                    pe.wait_ge(bank_read[k], q)
                a_hi, a_lo = OP[op]
                for kt in range(k_tiles):
                    if ready is not None:
                        ready(kt)
                    wh, wl = w_hi[k][:, kt * P:(kt + 1) * P], w_lo[k][:, kt * P:(kt + 1) * P]
                    ah, al = a_hi[:, kt * S:(kt + 1) * S], a_lo[:, kt * S:(kt + 1) * S]
                    pe.matmul(ps[k][:, :], wh, ah, start=(kt == 0), stop=False)
                    pe.matmul(ps[k][:, :], wh, al, start=False, stop=False)
                    mm = pe.matmul(ps[k][:, :], wl, ah, start=False, stop=(kt == k_tiles - 1))
                mm.then_inc(tile_done, 1)

            def made(base):
                return lambda kt: pe.wait_ge(operand, base + kt + 1)

            def quads(name, op, base, n=2):
                with pe.Fori(0, n) as i:
                    for k in range(4):
                        stream_tile(F[name] + i, k, op, made(base) if k == 0 else None)

            def turn(dst, src, signal):
                for b in range(NBLK):
                    mm = pe.transpose(dst[:, b * P:(b + 1) * P], src[:, b * P:(b + 1) * P], ident[:, :])
                mm.then_inc(signal, 1)

            def sum_squares(norm):
                pe.wait_ge(sum_added, 9 * NORM[norm] + 9)
                pe.matmul(aux[0][:, :], mean_d[:, :], ssum[:, :], start=True, stop=True).then_inc(norm_summed, 1)

            pe.wait_ge(consts, 8)
            pe.wait_ge(vec_loaded, 16 * 16)
            vec = vec_rows.rearrange("p (g c) -> p g c", g=4)
            for g, n in enumerate((80, 78, P, 3 * F2T - P + F2T)):
                mm = pe.transpose(aux[0][:, g * P:g * P + n], vec[0:n, g, :], ident[0:n, 0:n])
            mm.then_inc(rows_turned, 1)
            pe.wait_ge(ws_loaded, 16)
            for g in range(8):
                mm = pe.transpose(aux[1 + g // 4][:, g % 4 * P:(g % 4 + 1) * P], ws_rows[:, g * P:(g + 1) * P], ident[:, :])
            mm.then_inc(ws_turned, 1)
            pe.wait_ge(x_loaded, 16)
            for d in range(KT):
                bank = aux[3] if d % 2 == 0 else ps[3]
                if d >= 2:
                    pe.wait_ge(x_kept, d - 1)
                for b in range(NBLK):
                    mm = pe.transpose(bank[:, b * P:(b + 1) * P], gates[:, b * D + d * P:b * D + (d + 1) * P], ident[:, :])
                mm.then_inc(x_turned, 1)
            pe.wait_ge(table_kept, 1)
            sum_squares("n1")

            def v_turn(n):
                pe.wait_ge(bank_read[n % 4], n // 4 + 1)
                if n >= 2:
                    pe.wait_ge(v_kept, n - 1)
                turn(aux[n % 2], tb(n % 2), v_turned)

            def mix(g):
                if g == 0:
                    pe.wait_ge(ws_kept, 3)
                    pe.wait_ge(v_normed, NBLK)
                if g >= 2:
                    pe.wait_ge(mix_biased, g - 1)
                for b in range(NBLK):
                    mm = pe.matmul(aux[g % 2][:, b * P:(b + 1) * P], kept[:, b * D + g * P:b * D + (g + 1) * P],
                                   mixw[:, g * P:(g + 1) * P], start=True, stop=True)
                mm.then_inc(mixed, 1)

            for n in range(8):
                stream_tile(n // 4, n % 4, 0, made(MADE["n1"]) if n == 0 else None)
                if n >= 1:
                    v_turn(n - 1)
            for n in range(8):
                stream_tile(F["u"] + n // 4, n % 4, 0, None)
                if n == 0:
                    v_turn(7)
                if n >= 3:
                    mix(n - 3)
            for g in range(5, 8):
                mix(g)
            quads("ga", 0, MADE["n1"])
            quads("pa", 1, MADE["u"])
            quads("cg", 0, MADE["n1"])
            quads("xs", 0, MADE["n1"])
            quads("bg", 0, MADE["n1"])
            quads("gb", 0, MADE["n1"])
            quads("pb", 1, MADE["bg"])
            quads("out", 0, MADE["pb"])
            sum_squares("n2")

            def ada_turn(piece):
                pe.wait_ge(ada_step, 1 + KT * piece)
                for m in range(3):
                    mm = pe.matmul(aux[3][:, bass.ds(3 * piece + m, 1)], acc[:, m * P:(m + 1) * P], one[:, :],
                                   start=True, stop=True)
                mm.then_inc(ada_turned, 1)

            with pe.Fori(0, 4) as c:
                for part in range(2):
                    with pe.Fori(0, 2) as i:
                        base = MADE["n2"] if part == 0 else MADE["ff"] + KT * c
                        for k in range(4):
                            stream_tile(F["ff"] + 4 * c + 2 * part + i, k, 1 - part, made(base) if k == 0 else None)
                            if k == 1:
                                ada_turn(4 * c + 2 * part + i)
            ada_turn(16)
            sum_squares("between")
            sum_squares("n3")

            def fill(event, work):
                if AUX2[event] > 0:
                    pe.wait_ge(aux2_read, AUX2[event])
                work().then_inc(aux2_filled, 1)

            def turn_into_aux2(src):
                for b in range(NBLK):
                    mm = pe.transpose(aux[2][:, b * P:(b + 1) * P], src[:, b * P:(b + 1) * P], ident[:, :])
                return mm

            def low_rank():
                pe.wait_ge(gf_lo, 1)
                for kt in range(KT):
                    wh, wl = hi0[:, kt * P:(kt + 1) * P], lo0[:, kt * P:(kt + 1) * P]
                    ah, al = hi1[:, kt * S:(kt + 1) * S], lo1[:, kt * S:(kt + 1) * S]
                    pe.matmul(aux[2][:, :], wh, ah, start=(kt == 0), stop=False)
                    pe.matmul(aux[2][:, :], wh, al, start=False, stop=False)
                    mm = pe.matmul(aux[2][:, :], wl, ah, start=False, stop=(kt == KT - 1))
                return mm

            def chunk_products(r):
                pair, par = r // 2, r % 2
                half = slice(par * CHUNK, (par + 1) * CHUNK)
                for b in range(NBLK):
                    for e in range(2):
                        h = 2 * pair + e
                        mm = pe.matmul(aux[2][e * DK:(e + 1) * DK, b * P:(b + 1) * P],
                                       k_tok[half, b * 2 * P + h * DK:b * 2 * P + (h + 1) * DK],
                                       gv_tok[half, b * S + h * DV:b * S + (h + 1) * DV], start=True, stop=True)
                return mm

            def read_states(h):
                part = slice(h % 2 * DK, (h % 2 + 1) * DK)
                for n in range(NCH):
                    st = (h // 2 * NCH + n) * DV
                    mm = pe.matmul(aux[2][:, n * CHUNK:(n + 1) * CHUNK], states[part, st:st + DV],
                                   gq[h // 2][part, n * CHUNK:(n + 1) * CHUNK], start=True, stop=True)
                return mm

            for event in MIXER:
                kind, n = event
                if kind == "tile":
                    stream_tile(MIX_Q + n // 4, n % 4, 1, made(MADE["n3"]) if n == 0 else None)
                elif kind == "turn_v":
                    pe.wait_ge(bank_read[n], MIX_Q + 1)
                    fill(event, lambda: turn_into_aux2(tb(n % 2)))
                elif kind == "turn_gv":
                    pe.wait_ge(bank_read[n], MIX_Q + 5)
                    fill(event, lambda: turn_into_aux2(tb(n % 2)))
                elif kind == "fg" and n == 0:
                    fill(event, low_rank)
                elif kind == "fg":
                    if n == 1:
                        pe.wait_ge(small_loaded, 48)
                    fill(event, lambda: pe.matmul(aux[2][:, :], wfg[:, (n - 1) * P:n * P], gf_t, start=True, stop=True))
                elif kind == "turn_k":
                    pe.wait_ge(k_dec, n + 1)
                    fill(event, lambda: turn_into_aux2(gate_y[n]))
                elif kind == "kv":
                    fill(event, lambda: chunk_products(n))
                elif kind == "o":
                    pe.wait_ge(g_state, (NCH - 1) * (n // 2 + 1))
                    fill(event, lambda: read_states(n))
                elif kind == "ms":
                    pe.wait_ge(o_sq, n + 1)
                    fill(event, lambda: pe.matmul(aux[2][:, :], mean_h[:, :], tb(n % 2), start=True, stop=True))
                elif kind == "z":
                    h, i, t0, width = item(n)
                    part = slice(h % 2 * SB_DIM, (h % 2 + 1) * SB_DIM)
                    if i == 3:
                        pe.wait_ge(bank_read[h // 2], MIX_Q + 3)
                    if n >= 2:
                        pe.wait_ge(w_exp, n - 1)
                    q_t, k_t = tile(gates, h // 2), tile(gates, 4 + h // 2)
                    pe.matmul(aux[n % 2][:, 0:width], k_t[part, t0:t0 + P], q_t[part, t0:S],
                              start=True, stop=True).then_inc(z_done, 1)
                elif kind == "tri":
                    h, i, t0, width = item(n)
                    pe.wait_ge(sp_done, n + 1)
                    mm = pe.matmul(aux[n % 2][:, 0:width], neg_tri[:, :], SP[n % 2][:, 0:width],
                                   start=False, stop=True, skip_group_check=True)
                    if i < 3:
                        pe.wait_ge(later_done, 3 * h + 3 - i)
                        mm = pe.matmul(aux[n % 2][:, P:width], neg_one[:, :], later[:, t0 + P:S],
                                       start=False, stop=True, skip_group_check=True)
                    mm.then_inc(tri_done, 1)
                elif kind == "pv":
                    h, i, t0, width = item(n)
                    pe.wait_ge(w_masked, n + 1)
                    if n == 0:
                        pe.wait_ge(aux2_read, AUX2[("turn_v", 3)] + 1)
                    if i == 3 and h % 2 == 0 and h > 0:
                        pe.wait_ge(attn_lo, h // 2)
                    part = slice(h % 2 * SB_DIM, (h % 2 + 1) * SB_DIM)
                    pe.matmul(aux[3][part, t0:S], v_tok[:, i * S + h * SB_DIM:i * S + (h + 1) * SB_DIM],
                              E[n % 3][:, 0:width], start=(i == 3), stop=True,
                              skip_group_check=True).then_inc(pv_done, 1)

            def mixer_made(kt):
                if kt < 4:
                    pe.wait_ge(attn_lo, kt + 1)
                else:
                    pe.wait_ge(operand, MADE["gla"] + kt - 3)

            with pe.Fori(0, 2) as i:
                for k in range(4):
                    stream_tile(F["out2"] + i, k, 0, mixer_made if k == 0 else None)
            sum_squares("n4")
            with pe.Fori(0, 2) as c:
                with pe.Fori(0, 4) as i:
                    for k in range(4):
                        stream_tile(F["mlp"] + 6 * c + i, k, 1, made(MADE["n4"]) if k == 0 else None)
                with pe.Fori(0, 2) as i:
                    for k in range(4):
                        stream_tile(F["mlp"] + 6 * c + 4 + i, k, 0, made(MADE["mlp"] + KT * c) if k == 0 else None)
            quads("last_up", 1, MADE["n4"], 3)
            with pe.Fori(0, 2) as i:
                for k in range(4):
                    stream_tile(F["last_down"] + i, k, 0, made(MADE["last"]) if k == 0 else None, LAST_K)
            sum_squares("final")
            for n in range(KT):
                pe.wait_ge(value, VALUED["final"] + n + 1)
                if n >= 2:
                    pe.wait_ge(out_kept, n - 1)
                turn(aux[1 + n % 2], tA[n % 2], out_turned)

        @block.scalar
        def _(act):
            def weights(q, k, k_tiles=KT):
                if k % 2 == 0:
                    act.wait_ge(raw_landed[k // 2], 16 * (q + 1))
                if not (isinstance(q, int) and q == 0):
                    act.wait_ge(tile_done, 4 * (q - 1) + k + 1)
                src = raw[k // 2][:, 0:k_tiles * UNIT].rearrange("p (k n) -> p k n", n=UNIT)
                act.activation(w_hi[k][:, 0:k_tiles * P].rearrange("p (k n) -> p k n", n=P),
                               src[:, :, k % 2 * P:(k % 2 + 1) * P], ACT.Copy).then_inc(w_hi_done, 1)

            def round_operand(op, n, src, shift=None):
                if shift is None:
                    act.activation(tile(OP[op][0], n), src, ACT.Copy).then_inc(act_hi, 1)
                else:
                    act.activation(tile(OP[op][0], n), src, ACT.Identity, bias=shift).then_inc(act_hi, 1)

            def square(norm, n, slot):
                act.wait_ge(sum_added, 9 * NORM[norm] + max(n, 1))
                act.activation(tb(slot), tile(x, n), ACT.Square).then_inc(sq_done, 1)

            def norm(name, op, shift=None):
                act.wait_ge(norm_summed, NORM[name] + 1)
                act.activation(rinv[:, :], aux[0][:, :], ACT.Sqrt, bias=epsc[:, :]).then_inc(rms_done, 1)
                if op is not None:
                    for n in range(KT):
                        act.wait_ge(value, VALUED[name] + n + 1)
                        round_operand(op, n, tA[n % 2][:, :], None if shift is None else mod[:, shift + n:shift + n + 1])

            act.wait_ge(consts, 8)
            act.wait_ge(table_kept, 1)
            act.activation(cvec[:, :], col(C_C, KT), ACT.Silu).then_inc(c_ready, 1)
            for d in range(KT):
                act.wait_ge(x_kept, d + 1)
                square("n1", d, d % 2)
            for k in range(4):
                weights(0, k)
            norm("n1", 0)
            for n in range(8):
                q, k = n // 4, n % 4
                act.wait_ge(tile_done, n + 1)
                if n >= 2:
                    act.wait_ge(v_turned, n - 1)
                act.activation(tb(n % 2), ps[k][:, :], ACT.Gelu).then_inc(bank_read[k], 1)
                weights(q + 1, k)
            for n in range(8):
                q, k = F["u"] + n // 4, n % 4
                if n == 1:
                    act.wait_ge(v_kept, 8)
                    for b in range(NBLK):
                        if b > 0:
                            act.wait_ge(v_sumsq, b)
                        act.activation(tB[:, :], kept[:, b * D:(b + 1) * D], ACT.Square,
                                       accum_out=stat[:, b:b + 1]).then_inc(v_sumsq, 1)
                    act.wait_ge(v_sumsq, NBLK)
                    act.activation(stat[:, NBLK:2 * NBLK], stat[:, 0:NBLK], ACT.Sqrt, bias=epsc[:, :],
                                   scale=1.0 / D).then_inc(v_rms, 1)
                act.wait_ge(tile_done, 4 * q + k + 1)
                act.activation(tile(gates, n), ps[k][:, :], ACT.Gelu).then_inc(bank_read[k], 1)
                weights(q + 1, k)
                if n >= 3:
                    act.wait_ge(value, VALUED["u"] + n - 2)
                    round_operand(1, n - 3, tA[(n - 3) % 2][:, :])
            for n in range(5, 8):
                act.wait_ge(value, VALUED["u"] + n + 1)
                round_operand(1, n, tA[n % 2][:, :])

            def phase(name, work, n=2):
                with act.Fori(0, n) as i:
                    for k in range(4):
                        q = F[name] + i
                        act.wait_ge(tile_done, 4 * q + k + 1)
                        work(4 * i + k, q, k)
                        weights(q + 1, k)

            def sigmoid(c0):
                return lambda n, q, k: act.activation(tile(gates, n), ps[k][:, :], ACT.Sigmoid,
                                                      bias=col(c0 + n)).then_inc(bank_read[k], 1)

            def to_operand(op):
                def work(n, q, k):
                    act.wait_ge(bank_read[k], q + 1)
                    round_operand(op, n, tA[k % 2][:, :])
                return work

            def scale_last_tap(n, q, k):
                act.wait_ge(bank_read[k], q + 1)
                act.activation(tile(gates, n), tA[k % 2][:, :], ACT.Copy, scale=col(C_CONV + 2 * KT + n)).then_inc(tap0, 1)

            def projected(n, q, k):
                act.wait_ge(value, VALUED["pb"] + n + 1)
                round_operand(0, n, tA[k % 2][:, :])

            def square_x(name):
                def work(n, q, k):
                    act.wait_ge(bank_read[k], q + 1)
                    act.wait_ge(sum_added, 9 * NORM[name] + n)
                    act.activation(tb(k % 2), tile(x, n), ACT.Square).then_inc(sq_done, 1)
                return work

            nothing = lambda n, q, k: None
            phase("ga", sigmoid(C_BGATE))
            phase("pa", nothing)
            phase("cg", lambda n, q, k: act.activation(tile(gates, n), ps[k][:, :], ACT.Copy).then_inc(bank_read[k], 1))
            phase("xs", scale_last_tap)
            phase("bg", to_operand(1))
            phase("gb", sigmoid(C_BGATE + KT))
            phase("pb", projected)
            phase("out", square_x("n2"))
            norm("n2", 1)

            def ff_chunk(c, last):
                for part in range(2):
                    with act.Fori(0, 2) as i:
                        for k in range(4):
                            q = F["ff"] + 4 * c + 2 * part + i
                            act.wait_ge(tile_done, 4 * q + k + 1)
                            if part == 0:
                                act.activation(tb(k % 2), ps[k][:, :], ACT.Relu).then_inc(bank_read[k], 1)
                                act.wait_ge(value, VALUED["ff"] + KT * c + 4 * i + k + 1)
                                round_operand(0, 4 * i + k, tA[k % 2][:, :])
                            elif last:
                                square_x("between")(4 * i + k, q, k)
                            weights(q + 1, k)

            with act.Fori(0, 3) as c:
                ff_chunk(c, False)
            ff_chunk(3, True)
            norm("between", None)
            for n in range(KT):
                act.wait_ge(x_kept, KT + n + 1)
                square("n3", n, n % 2)
            act.wait_ge(small_loaded, 48)
            act.wait_ge(gf_zeroed, 2)
            act.activation(hi0[:, 0:KT * P].rearrange("p (k n) -> p k n", n=P)[:, :, 0:RANK],
                           raw_gf[:, :].rearrange("p (k n) -> p k n", n=RANK), ACT.Copy).then_inc(gf_hi, 1)
            norm("n3", 1, 0)

            for event in MIXER:
                kind, n = event
                if kind == "tile":
                    q, k = MIX_Q + n // 4, n % 4
                    act.wait_ge(tile_done, 4 * q + k + 1)
                    if n < 4 or 16 <= n < 20:
                        if n < 4 and n >= 2:
                            act.wait_ge(aux2_filled, AUX2[("turn_v", n - 2)] + 1)
                        if n >= 18:
                            act.wait_ge(aux2_filled, AUX2[("turn_gv", n - 18)] + 1)
                        act.activation(tb(n % 2), ps[k][:, :], ACT.Copy).then_inc(bank_read[k], 1)
                    elif n < 8:
                        act.activation(tile(gates, n - 4), ps[k][:, :], ACT.Copy, scale=SB_DIM ** -0.5).then_inc(bank_read[k], 1)
                    elif n < 12:
                        act.activation(tile(gates, n - 4), ps[k][:, :], ACT.Copy).then_inc(bank_read[k], 1)
                    elif n < 14:
                        act.activation(gq[n - 12], ps[k][:, :], ACT.Copy, scale=DK ** -0.5).then_inc(bank_read[k], 1)
                    elif n < 16:
                        act.activation(gk[n - 14], ps[k][:, :], ACT.Copy).then_inc(bank_read[k], 1)
                    else:
                        act.activation(yb[:, (n - 20) * S:(n - 19) * S], ps[k][:, :], ACT.Silu).then_inc(bank_read[k], 1)
                    weights(q + 1, k)
                elif kind == "fg" and n > 0:
                    p = n - 1
                    act.wait_ge(g_abs, p + 1)
                    act.activation(gate_e[p], gate_e[p], ACT.Exp, scale=-1.0).then_inc(g_exp, 1)
                    act.wait_ge(g_exp, p + 1)
                    act.activation(gate_e[p], gate_e[p], ACT.Ln, bias=one[:, :]).then_inc(g_log, 1)
                    act.wait_ge(g_rest, p + 1)
                    act.activation(decay[:, p * NCH:(p + 1) * NCH], gate_e[p][:, CHUNK - 1:S:CHUNK], ACT.Exp,
                                   scale=-1.0 / TAU).then_inc(g_dec, 1)
                    act.activation(gate_y[p], gate_y[p], ACT.Exp, scale=-1.0 / TAU).then_inc(g_dec, 1)
                elif kind == "o":
                    act.wait_ge(aux2_filled, AUX2[event] + 1)
                    act.activation(tb(n % 2), aux[2][:, :], ACT.Square).then_inc(o_sq, 1)
                elif kind == "ms":
                    act.wait_ge(aux2_filled, AUX2[event] + 1)
                    act.activation(tb(n % 2), aux[2][:, :], ACT.Sqrt, bias=epsc[:, :]).then_inc(aux2_read, 1)
                    act.wait_ge(value, VALUED["gla"] + n + 1)
                    round_operand(0, 4 + n, tA[n % 2][:, :])
                elif kind == "z":
                    width = item(n)[3]
                    e = E[n % 3][:, 0:width]
                    act.wait_ge(z_done, n + 1)
                    if n >= 3:
                        act.wait_ge(pv_done, n - 2)
                    act.activation(e, aux[n % 2][:, 0:width], ACT.Abs).then_inc(z_abs, 1)
                    act.wait_ge(z_abs, n + 1)
                    act.activation(e, e, ACT.Exp, scale=-1.0).then_inc(z_exp, 1)
                    act.wait_ge(z_exp, n + 1)
                    act.activation(e, e, ACT.Ln, bias=one[:, :]).then_inc(z_log, 1)
                elif kind == "tri":
                    width = item(n)[3]
                    act.wait_ge(tri_done, n + 1)
                    act.activation(E[n % 3][:, 0:width], aux[n % 2][:, 0:width], ACT.Exp).then_inc(w_exp, 1)
                elif kind == "pv" and n % 8 == 7:
                    act.wait_ge(pv_done, n + 1)
                    act.activation(tile(hi0, n // 8), aux[3][:, :], ACT.Copy).then_inc(attn_hi, 1)

            phase("out2", square_x("n4"))
            norm("n4", 1, 3 * KT)

            def up_tile(q, k, val, n, conv_count, silu_count, value_count):
                ct = val if k < 2 else F2T // 2 + val
                act.activation(yb[:, k * S:(k + 1) * S], ps[k][:, :], ACT.Identity, bias=col(C_BCONV + ct),
                               scale=col(C_WCONV + 2 * F2T + ct)).then_inc(tap0, 1)
                return ct

            def up(q, i, c0, value_base, k_next=KT):
                for k in range(4):
                    act.wait_ge(tile_done, 4 * q + k + 1)
                    up_tile(q, k, c0 + k % 2, None, None, None, None)
                    weights(q + 1, k, k_next)
                    if k >= 2:
                        act.wait_ge(bank_read[k], q + 1)
                        act.activation(tb(k - 2), yb[:, k * S:(k + 1) * S], ACT.Silu).then_inc(silu_done, 1)
                        act.wait_ge(value, value_base + k - 1)
                        round_operand(0, 2 * i + k - 2, tA[k - 2][:, :])

            with act.Fori(0, 2) as c:
                with act.Fori(0, 4) as i:
                    up(F["mlp"] + 6 * c + i, i, KT * c + 2 * i, VALUED["mlp"] + KT * c + 2 * i)
                with act.Fori(0, 2) as i:
                    for k in range(4):
                        weights(F["mlp"] + 6 * c + 4 + i + 1, k)
            for i in range(3):
                up(F["last_up"] + i, i, 2 * KT + 2 * i, VALUED["last"] + 2 * i, LAST_K if i == 2 else KT)
            for i in range(2):
                for k in range(4):
                    square_x("final")(4 * i + k, F["last_down"] + i, k)
                    if i == 0:
                        weights(F["last_down"] + 1, k, LAST_K)
            norm("final", None)
            for n in range(KT):
                act.wait_ge(out_turned, n + 1)
                act.activation(gates[:, :].rearrange("p (b n) -> p b n", b=NBLK)[:, :, n * P:(n + 1) * P],
                               aux[1 + n % 2][:, :].rearrange("p (b n) -> p b n", b=NBLK), ACT.Copy).then_inc(out_kept, 1)

        @block.vector
        def _(dve):
            def weights(q, k, k_tiles=KT):
                dve.wait_ge(w_hi_done, 4 * q + k + 1)
                src = raw[k // 2][:, 0:k_tiles * UNIT].rearrange("p (k n) -> p k n", n=UNIT)
                dve.tensor_tensor(w_lo[k][:, 0:k_tiles * P].rearrange("p (k n) -> p k n", n=P),
                                  src[:, :, k % 2 * P:(k % 2 + 1) * P],
                                  w_hi[k][:, 0:k_tiles * P].bitcast(F32).rearrange("p (k n) -> p k n", n=P),
                                  ALU.subtract).then_inc(w_lo_done, 1)

            def rest(op, n, src, made_before, shift=None):
                dve.wait_ge(act_hi, made_before + 1)
                hi, lo = tile(OP[op][0], n).bitcast(F32), tile(OP[op][1], n)
                if shift is None:
                    dve.tensor_tensor(lo, src, hi, ALU.subtract).then_inc(operand, 1)
                else:
                    dve.scalar_tensor_tensor(out=lo, in0=src, scalar=shift, in1=hi, op0=ALU.add,
                                             op1=ALU.subtract).then_inc(operand, 1)
                dve.wait_ge(operand, made_before + 1)

            def clear_sum():
                dve.memset(ssum[:, :], 0.0).then_inc(sum_added, 1)

            def add_square(name, n, slot):
                count = NORM[name]
                dve.wait_ge(sq_done, 8 * count + n + 1)
                dve.wait_ge(sum_added, 9 * count + n + 1)
                dve.tensor_tensor(ssum[:, :], ssum[:, :], tb(slot), ALU.add).then_inc(sum_added, 1)

            def invert_rms(name):
                dve.wait_ge(rms_done, NORM[name] + 1)
                dve.reciprocal(rinv[:, :], rinv[:, :]).then_inc(inv_done, 1)
                dve.wait_ge(inv_done, NORM[name] + 1)

            def norm(name, op, gain, shift=None):
                invert_rms(name)

                def split(n):
                    rest(op, n, tA[n % 2][:, :], MADE[name] + n, None if shift is None else mod[:, shift + n:shift + n + 1])

                for n in range(KT):
                    if op is None and n >= 2:
                        dve.wait_ge(out_turned, n - 1)
                    dve.scalar_tensor_tensor(out=tA[n % 2][:, :], in0=tile(x, n), scalar=gain(n), in1=rinv[:, :],
                                             op0=ALU.mult, op1=ALU.mult).then_inc(value, 1)
                    if op is not None and n >= 1:
                        split(n - 1)
                if op is not None:
                    split(KT - 1)

            clear_sum()
            dve.memset(acc[:, :], 0.0).then_inc(ada_step, 1)
            dve.wait_ge(rows_turned, 1)
            dve.tensor_copy(table[:, 0:80], aux[0][:, 0:80])
            dve.tensor_copy(table[:, 128:206], aux[0][:, 128:206])
            dve.tensor_copy(table[:, 256:432], aux[0][:, 256:432]).then_inc(table_kept, 1)
            dve.wait_ge(ws_turned, 1)
            wv = mixw[:, :].rearrange("p (g i) -> p g i", g=8)
            for g in range(2):
                src = aux[1 + g][:, :].rearrange("p (g i) -> p g i", g=4)
                dve.tensor_copy(wv[:, 4 * g:4 * g + 4, :], src).then_inc(ws_kept, 1)
            dve.wait_ge(ws_kept, 2)
            dve.memset(wv[CHUNK:P, :, 0:CHUNK], 0.0).then_inc(ws_kept, 1)
            for d in range(KT):
                dve.wait_ge(x_turned, d + 1)
                bank = aux[3] if d % 2 == 0 else ps[3]
                dve.tensor_copy(tile(x, d), bank[:, :]).then_inc(x_kept, 1)
                if d >= 1:
                    add_square("n1", d - 1, (d - 1) % 2)
            add_square("n1", KT - 1, 1)
            for k in range(4):
                weights(0, k)
            dve.wait_ge(table_kept, 1)
            norm("n1", 0, lambda n: col(C_NMIX + n))

            def keep_v(n):
                dve.wait_ge(v_turned, n + 1)
                dve.tensor_copy(kept[:, :].rearrange("p (b n) -> p b n", b=NBLK)[:, :, n * P:(n + 1) * P],
                                aux[n % 2][:, :].rearrange("p (b n) -> p b n", b=NBLK)).then_inc(v_kept, 1)

            def mixed_value(g):
                if g == 0:
                    dve.wait_ge(small_loaded, 48)
                dve.wait_ge(mixed, g + 1)
                bias = mixb[:, g * P:(g + 1) * P].unsqueeze(1).to_broadcast([P, NBLK, P])
                dve.scalar_tensor_tensor(out=tA[g % 2][:, :].rearrange("p (b n) -> p b n", b=NBLK),
                                         in0=aux[g % 2][:, :].rearrange("p (b n) -> p b n", b=NBLK),
                                         scalar=col(C_NV + g), in1=bias, op0=ALU.mult, op1=ALU.add).then_inc(mix_biased, 1)
                dve.wait_ge(mix_biased, g + 1)
                dve.wait_ge(bank_read[g % 4], F["u"] + g // 4 + 1)
                dve.tensor_tensor(tA[g % 2][:, :], tA[g % 2][:, :], tile(gates, g), ALU.mult).then_inc(value, 1)
                rest(1, g, tA[g % 2][:, :], MADE["u"] + g)

            for n in range(8):
                if n >= 1:
                    weights((n - 1) // 4 + 1, (n - 1) % 4)
                if n >= 1:
                    keep_v(n - 1)
            weights(2, 3)
            for n in range(8):
                q, k = F["u"] + n // 4, n % 4
                if n == 0:
                    keep_v(7)
                if n == 1:
                    dve.wait_ge(v_rms, 1)
                    dve.reciprocal(stat[:, 2 * NBLK:3 * NBLK], stat[:, NBLK:2 * NBLK]).then_inc(v_inv, 1)
                    dve.wait_ge(v_inv, 1)
                    for b in range(NBLK):
                        dve.tensor_scalar(kept[:, b * D:(b + 1) * D], kept[:, b * D:(b + 1) * D],
                                          stat[:, 2 * NBLK + b:2 * NBLK + b + 1], None, ALU.mult).then_inc(v_normed, 1)
                weights(q + 1, k)
                if n >= 3:
                    mixed_value(n - 3)
            for g in range(5, 8):
                mixed_value(g)

            def phase(name, work, after=None, n=2):
                with dve.Fori(0, n) as i:
                    for k in range(4):
                        q = F[name] + i
                        if work is not None:
                            dve.wait_ge(tile_done, 4 * q + k + 1)
                            work(4 * i + k, q, k)
                        if after is not None:
                            after(4 * i + k, q, k)
                        weights(q + 1, k)

            def product(dst, src):
                def work(n, q, k):
                    dve.tensor_tensor(dst(n, k), ps[k][:, :], src(n), ALU.mult).then_inc(bank_read[k], 1)
                return work

            def to_value(n, k):
                return tA[k % 2][:, :]

            def taps(n, q, k):
                z, y = tA[k % 2], gates
                for j, (ready, signal) in enumerate(((tap0, tap1), (tap1, tap2))):
                    dve.wait_ge(ready, n + 1)
                    d = j + 1
                    yv = y[:, bass.ds(n * S + d, S - d)]
                    dve.scalar_tensor_tensor(out=yv, in0=z[:, 0:S - d], scalar=col(C_CONV + (1 - j) * KT + n), in1=yv,
                                             op0=ALU.mult, op1=ALU.add).then_inc(signal, 1)
                dve.wait_ge(tap2, n + 1)

            def gate_conv(n, q, k):
                dve.wait_ge(tap2, n + 1)
                product(to_value, lambda m: tile(gates, m))(n, q, k)

            def add_kept(n, q, k):
                dve.wait_ge(bank_read[k], q + 1)
                dve.tensor_tensor(tA[k % 2][:, :], tA[k % 2][:, :], tile(kept, n), ALU.add).then_inc(value, 1)
                rest(0, n, tA[k % 2][:, :], MADE["pb"] + n)

            def grow_x(n, q, k):
                dve.tensor_tensor(tile(x, n), tile(x, n), ps[k][:, :], ALU.add).then_inc(bank_read[k], 1)

            phase("ga", None)
            phase("pa", product(lambda n, k: tile(kept, n), lambda n: tile(gates, n)))
            phase("cg", None)
            phase("xs", product(to_value, lambda n: tile(gates, n)), taps)
            phase("bg", gate_conv, lambda n, q, k: rest(1, n, tA[k % 2][:, :], MADE["bg"] + n))
            phase("gb", None)
            phase("pb", product(to_value, lambda n: tile(gates, n)), add_kept)
            clear_sum()
            phase("out", grow_x, lambda n, q, k: add_square("n2", n, k % 2))
            norm("n2", 1, lambda n: col(C_NFF + n))

            def ff_chunk(c, last):
                if last:
                    clear_sum()
                for part in range(2):
                    with dve.Fori(0, 2) as i:
                        for k in range(4):
                            q = F["ff"] + 4 * c + 2 * part + i
                            n = 4 * i + k
                            piece = 4 * c + 2 * part + i
                            if part == 1:
                                dve.wait_ge(tile_done, 4 * q + k + 1)
                            if part == 0:
                                dve.wait_ge(bank_read[k], q + 1)
                                dve.tensor_tensor(tA[k % 2][:, :], tb(k % 2), tb(k % 2), ALU.mult).then_inc(value, 1)
                                rest(0, n, tA[k % 2][:, :], MADE["ff"] + KT * c + n)
                            else:
                                grow_x(n, q, k)
                                if last:
                                    add_square("between", n, k % 2)
                            weights(q + 1, k)
                            if k == 2:
                                dve.wait_ge(ada_landed, 16 * (piece + 1))
                                dve.wait_ge(ada_turned, piece + 1)
                            if k >= 2:
                                for kt in range(4 * (k - 2), 4 * (k - 1)):
                                    src = ada_raw[:, kt * ADA:(kt + 1) * ADA]
                                    if kt == 0:
                                        dve.tensor_scalar(acc[:, :], src, cvec[:, kt:kt + 1], None, ALU.mult)\
                                           .then_inc(ada_step, 1)
                                    else:
                                        dve.wait_ge(ada_step, 1 + KT * piece + kt)
                                        dve.scalar_tensor_tensor(out=acc[:, :], in0=src, scalar=cvec[:, kt:kt + 1],
                                                                 in1=acc[:, :], op0=ALU.mult, op1=ALU.add)\
                                           .then_inc(ada_step, 1)

            dve.wait_ge(c_ready, 1)
            with dve.Fori(0, 3) as c:
                ff_chunk(c, False)
            ff_chunk(3, True)

            invert_rms("between")
            clear_sum()
            for n in range(KT):
                dve.scalar_tensor_tensor(out=tile(x, n), in0=tile(x, n), scalar=col(C_NFIN + n), in1=rinv[:, :],
                                         op0=ALU.mult, op1=ALU.mult).then_inc(x_kept, 1)
                if n >= 1:
                    add_square("n3", n - 1, (n - 1) % 2)
            add_square("n3", KT - 1, (KT - 1) % 2)
            dve.memset(hi0[:, 0:KT * P].bitcast(F32), 0.0).then_inc(gf_zeroed, 1)
            dve.memset(lo0[:, 0:KT * P].bitcast(F32), 0.0).then_inc(gf_zeroed, 1)
            dve.wait_ge(ada_turned, 17)
            dve.tensor_tensor(mod[:, :], aux[3][:, 3:3 + NMOD * KT], col(C_BADA, NMOD * KT), ALU.add).then_inc(mod_done, 1)
            dve.wait_ge(mod_done, 1)
            for s, m, g in ((0, 1, C_G1), (1, 4, C_G2)):
                dve.scalar_tensor_tensor(out=scales[:, s * KT:(s + 1) * KT], in0=mod[:, m * KT:(m + 1) * KT], scalar=1.0,
                                         in1=col(g, KT), op0=ALU.add, op1=ALU.mult).then_inc(mod_done, 1)
            for s, m in ((2, 2), (3, 5)):
                dve.tensor_scalar(scales[:, s * KT:(s + 1) * KT], mod[:, m * KT:(m + 1) * KT], 1.0, None,
                                  ALU.add).then_inc(mod_done, 1)
            dve.wait_ge(gf_hi, 1)
            gf = raw_gf[:, :].rearrange("p (k n) -> p k n", n=RANK)
            dve.wait_ge(gf_zeroed, 2)
            dve.tensor_tensor(lo0[:, 0:KT * P].rearrange("p (k n) -> p k n", n=P)[:, :, 0:RANK], gf,
                              hi0[:, 0:KT * P].bitcast(F32).rearrange("p (k n) -> p k n", n=P)[:, :, 0:RANK],
                              ALU.subtract).then_inc(gf_lo, 1)
            dve.wait_ge(mod_done, 5)
            norm("n3", 1, lambda n: scales[:, n:n + 1], 0)
            dve.memset(rinv[:, :], 1.0).then_inc(reset_ready, 1)
            dve.wait_ge(reset_ready, 1)
            dve.memset(rinv[:, 0:S:CHUNK], 0.0).then_inc(reset_ready, 1)

            def keep_turned(event, dst):
                dve.wait_ge(aux2_filled, AUX2[event] + 1)
                dve.tensor_copy(dst, aux[2][:, :].rearrange("p (b n) -> p b n", b=NBLK)).then_inc(aux2_read, 1)

            def softplus_gate(p, event):
                y, e = gate_y[p], gate_e[p]
                dve.wait_ge(aux2_filled, AUX2[event] + 1)
                dve.tensor_scalar(y, aux[2][:, :], col(C_BFG + p), -1.0, ALU.add, ALU.mult).then_inc(aux2_read, 1)
                dve.wait_ge(aux2_read, AUX2[event] + 1)
                dve.scalar_tensor_tensor(out=e, in0=y, scalar=-1.0, in1=y, op0=ALU.mult, op1=ALU.max).then_inc(g_abs, 1)
                dve.wait_ge(g_log, p + 1)
                dve.scalar_tensor_tensor(out=y, in0=y, scalar=0.0, in1=e, op0=ALU.max, op1=ALU.add).then_inc(g_sp, 1)
                dve.wait_ge(g_sp, p + 1)
                dve.wait_ge(reset_ready, 2)
                dve.tensor_tensor_scan(e, rinv[:, :], y, 0.0, ALU.mult, ALU.add).then_inc(g_cum, 1)
                dve.wait_ge(g_cum, p + 1)
                ev = e.rearrange("p (c s) -> p c s", s=CHUNK)
                dve.tensor_tensor(y.rearrange("p (c s) -> p c s", s=CHUNK),
                                  ev[:, :, CHUNK - 1:CHUNK].to_broadcast([P, NCH, CHUNK]), ev,
                                  ALU.subtract).then_inc(g_rest, 1)

            for event in MIXER:
                kind, n = event
                if kind == "tile":
                    weights(MIX_Q + n // 4 + 1, n % 4)
                elif kind == "turn_v":
                    keep_turned(event, v_tok.rearrange("p (b n) -> p b n", b=NBLK)[:, :, n * P:(n + 1) * P])
                elif kind == "turn_gv":
                    keep_turned(event, gv_tok.rearrange("p (b n) -> p b n", b=NBLK)[:, :, n * P:(n + 1) * P])
                elif kind == "turn_k":
                    dve.wait_ge(g_dec, 2 * n + 2)
                    dve.wait_ge(bank_read[2 + n], MIX_Q + 4)
                    dve.tensor_tensor(gate_y[n], gk[n], gate_y[n], ALU.mult).then_inc(k_dec, 1)
                    keep_turned(event, k_tok.rearrange("p (b n) -> p b n", b=NBLK)[:, :, n * P:(n + 1) * P])
                elif kind == "fg" and n == 0:
                    dve.wait_ge(aux2_filled, AUX2[event] + 1)
                    dve.tensor_copy(gf_t, aux[2][0:RANK, :]).then_inc(aux2_read, 1)
                elif kind == "fg":
                    softplus_gate(n - 1, event)
                elif kind == "kv":
                    pair, par = n // 2, n % 2
                    if n == 0:
                        dve.wait_ge(tile_done, 4 * (MIX_Q + 5) + 4)
                    dve.wait_ge(aux2_filled, AUX2[event] + 1)
                    dst = states[:, pair * NCH * DV:(pair + 1) * NCH * DV].rearrange("p (b c n) -> p b c n", c=2, n=DV)
                    dve.tensor_copy(dst[:, :, par, :], aux[2][:, :].rearrange("p (b n) -> p b n", b=NBLK)).then_inc(aux2_read, 1)
                    if par == 1:
                        dve.wait_ge(aux2_read, AUX2[event] + 1)
                        for c in range(1, NCH):
                            st = (pair * NCH + c) * DV
                            if c > 1:
                                dve.wait_ge(g_state, (NCH - 1) * pair + c - 1)
                            dve.scalar_tensor_tensor(out=states[:, st:st + DV], in0=states[:, st - DV:st],
                                                     scalar=decay[:, pair * NCH + c:pair * NCH + c + 1],
                                                     in1=states[:, st:st + DV], op0=ALU.mult, op1=ALU.add).then_inc(g_state, 1)
                elif kind == "o":
                    dve.wait_ge(o_sq, n + 1)
                    dve.tensor_scalar(tA[n % 2][:, :], aux[2][:, :], col(C_GGLA + n), None, ALU.mult).then_inc(aux2_read, 1)
                elif kind == "ms":
                    dve.wait_ge(aux2_read, AUX2[event] + 1)
                    dve.reciprocal(tb(n % 2), tb(n % 2)).then_inc(g_inv, 1)
                    dve.wait_ge(g_inv, n + 1)
                    dve.tensor_tensor(tA[n % 2][:, :], tA[n % 2][:, :], tb(n % 2), ALU.mult).then_inc(g_scaled, 1)
                    dve.wait_ge(g_scaled, n + 1)
                    dve.wait_ge(bank_read[n], MIX_Q + 6)
                    dve.tensor_tensor(tA[n % 2][:, :], tA[n % 2][:, :], yb[:, n * S:(n + 1) * S], ALU.mult).then_inc(value, 1)
                    rest(0, 4 + n, tA[n % 2][:, :], MADE["gla"] + n)
                elif kind == "z":
                    h, i, t0, width = item(n)
                    e, zb = E[n % 3][:, 0:width], aux[n % 2][:, 0:width]
                    dve.wait_ge(z_log, n + 1)
                    if n >= 2:
                        dve.wait_ge(tri_done, n - 1)
                    dve.scalar_tensor_tensor(out=SP[n % 2][:, 0:width], in0=zb, scalar=0.0, in1=e, op0=ALU.max,
                                             op1=ALU.add).then_inc(sp_raw, 1)
                    dve.wait_ge(sp_raw, n + 1)
                    dve.tensor_tensor(SP[n % 2][:, 0:P], SP[n % 2][:, 0:P], before[:, :], ALU.mult).then_inc(sp_done, 1)
                elif kind == "tri":
                    h, i, t0, width = item(n)
                    if i > 0:
                        dve.wait_ge(tri_done, n + 1)
                        new = dve.tensor_copy(later[:, t0:t0 + P], SP[n % 2][:, 0:P])
                        if i < 3:
                            dve.tensor_tensor(later[:, t0 + P:S], later[:, t0 + P:S], SP[n % 2][:, P:width],
                                              ALU.add).then_inc(later_done, 1)
                        else:
                            new.then_inc(later_done, 1)
                        dve.wait_ge(later_done, 3 * h + 4 - i)
                elif kind == "pv" and n % 8 == 7:
                    dve.wait_ge(attn_hi, n // 8 + 1)
                    dve.tensor_tensor(tile(lo0, n // 8), aux[3][:, :], tile(hi0, n // 8).bitcast(F32),
                                      ALU.subtract).then_inc(attn_lo, 1)

            clear_sum()

            def grow_scaled(s):
                def work(n, q, k):
                    dve.scalar_tensor_tensor(out=tile(x, n), in0=ps[k][:, :], scalar=scales[:, bass.ds(s * KT + n, 1)],
                                             in1=tile(x, n), op0=ALU.mult, op1=ALU.add).then_inc(bank_read[k], 1)
                return work

            phase("out2", grow_scaled(2), lambda n, q, k: add_square("n4", n, k % 2))
            norm("n4", 1, lambda n: scales[:, KT + n:KT + n + 1], 3 * KT)

            def up(q, i, c0, done, made_base, k_next=KT):
                for k in range(4):
                    ct = c0 + k % 2 + (F2T // 2 if k >= 2 else 0)
                    y = yb[:, k * S:(k + 1) * S]
                    dve.wait_ge(tap0, KT + 4 * done + k + 1)
                    dve.scalar_tensor_tensor(out=y[:, 1:S], in0=ps[k][:, 0:S - 1], scalar=col(C_WCONV + F2T + ct),
                                             in1=y[:, 1:S], op0=ALU.mult, op1=ALU.add).then_inc(tap1, 1)
                    dve.wait_ge(tap1, KT + 4 * done + k + 1)
                    dve.scalar_tensor_tensor(out=y[:, 2:S], in0=ps[k][:, 0:S - 2], scalar=col(C_WCONV + ct),
                                             in1=y[:, 2:S], op0=ALU.mult, op1=ALU.add).then_inc(bank_read[k], 1)
                    weights(q + 1, k, k_next)
                    if k >= 2:
                        dve.wait_ge(silu_done, 2 * done + k - 1)
                        dve.wait_ge(bank_read[k - 2], q + 1)
                        dve.tensor_tensor(tA[k - 2][:, :], yb[:, (k - 2) * S:(k - 1) * S], tb(k - 2),
                                          ALU.mult).then_inc(value, 1)
                        rest(0, 2 * i + k - 2, tA[k - 2][:, :], made_base + 2 * i + k - 2)

            with dve.Fori(0, 2) as c:
                with dve.Fori(0, 4) as i:
                    up(F["mlp"] + 6 * c + i, i, KT * c + 2 * i, 4 * c + i, MADE["mlp"] + KT * c)
                with dve.Fori(0, 2) as i:
                    for k in range(4):
                        q = F["mlp"] + 6 * c + 4 + i
                        dve.wait_ge(tile_done, 4 * q + k + 1)
                        grow_scaled(3)(4 * i + k, q, k)
                        weights(q + 1, k)
            for i in range(3):
                up(F["last_up"] + i, i, 2 * KT + 2 * i, 8 + i, MADE["last"], LAST_K if i == 2 else KT)
            clear_sum()
            for i in range(2):
                for k in range(4):
                    q = F["last_down"] + i
                    dve.wait_ge(tile_done, 4 * q + k + 1)
                    grow_scaled(3)(4 * i + k, q, k)
                    add_square("final", 4 * i + k, k % 2)
                    if i == 0:
                        weights(q + 1, k, LAST_K)
            norm("final", None, lambda n: col(C_GFIN + n))


INPUTS = ["x", "norm_mix_g", "w_in", "b_gate", "norm_v_g", "w_s", "b_s", "conv_w", "w_proj_a", "w_proj_b", "w_out",
          "norm_ff_g", "w_ff1", "w_ff2", "norm_final_g", "c_2", "w_ada_2", "b_ada_2", "g_norm1_2", "w_in_2", "w_fg2_2", "b_fg2_2",
          "g_gla_out_2", "w_out_2", "g_norm2_2", "w_up_2", "w_conv_2", "b_conv_2", "w_down_2", "g_final_2"]


def kernel(**inputs):
    import numpy as np
    from concourse import bacc
    from concourse.bass_utils import run_bass_kernel_spmd

    nc = bacc.Bacc("TRN2", target_bir_lowering=False, num_devices=1)
    arrays, aps = {}, {}
    for name in INPUTS:
        array = np.ascontiguousarray(inputs[name])
        arrays[f"in_{name}"] = array
        aps[name] = nc.dram_tensor(f"in_{name}", array.shape, mybir.dt.from_np(array.dtype), kind="ExternalInput").ap()
    out = nc.dram_tensor("out", (1, S, D), F32, kind="ExternalOutput").ap()
    build(nc, aps, out)
    result = run_bass_kernel_spmd(nc, [arrays], core_ids=[0])
    return result.results[0]["out"]
```

```python
from contextlib import ExitStack

import concourse.bass as bass
from concourse import mybir

P = 128
S = 512
D = 1024
KT = D // P
UNIT = 256
NBLK = S // P
EPS = 1e-6
F2 = 2816
SB_HEADS, SB_DIM = 8, 64
GLA_HEADS, DK, DV, CHUNK = 4, 64, 128, 64
NCH = S // CHUNK
RANK = 16
TAU = 16.0
NMOD = 6

F32 = mybir.dt.float32
F32R = mybir.dt.float32r
BF16 = mybir.dt.bfloat16
ALU = mybir.AluOpType
ACT = mybir.ActivationFunctionType

QUADS = [("v", 2), ("u", 2), ("ga", 2), ("pa", 2), ("cg", 2), ("xs", 2), ("bg", 2), ("gb", 2), ("pb", 2),
         ("out", 2), ("ff", 16), ("w2", 6), ("out2", 2), ("mlp", 12), ("last_up", 3), ("last_down", 2)]
FIRST = {}
for _name, _n in QUADS:
    FIRST[_name] = sum(n for _, n in QUADS[:len(FIRST)])
NQ = sum(n for _, n in QUADS)

OPERANDS = [("n1", 8), ("u", 8), ("bg", 8), ("pb", 8), ("n2", 8), ("ff", 32), ("n3", 8), ("gla", 4),
            ("n4", 8), ("mlp", 16), ("last", 6)]
MADE = {}
for _name, _n in OPERANDS:
    MADE[_name] = sum(n for _, n in OPERANDS[:len(MADE)])

VALUES = [(name, n) for name, n in OPERANDS if name != "bg"] + [("final", 8)]
VALUED = {}
for _name, _n in VALUES:
    VALUED[_name] = sum(n for _, n in VALUES[:len(VALUED)])

C_NMIX, C_BGATE, C_NV, C_CONV, C_NFF, C_C, C_NFIN = 0, 8, 24, 32, 56, 64, 72
C_BADA, C_G1, C_BFG, C_GGLA, C_G2, C_GFIN = 128, 176, 184, 186, 190, 198
C_WCONV, C_BCONV = 256, 388
F2T = 2 * F2 // P


ADA = 3 * P
N_ITEMS = 4 * SB_HEADS
Z_BOUND = 40.0


def mixer_schedule():
    order = [("tile", 0)]
    for t in range(1, 4):
        order += [("tile", t), ("turn_v", t - 1)]
    order += [("tile", 4), ("turn_v", 3)] + [("tile", t) for t in range(5, 9)]
    step = 0

    def attend(n=1):
        nonlocal step
        for _ in range(n):
            if step < N_ITEMS:
                order.append(("z", step))
            if 1 <= step <= N_ITEMS:
                order.append(("tri", step - 1))
            if 2 <= step <= N_ITEMS + 1:
                order.append(("pv", step - 2))
            step += 1

    gla = {(9, 2): [("fg", 0)], (10, 2): [("fg", 1)], (11, 2): [("fg", 2)], (16, 0): [("turn_k", 0)], (16, 1): [("turn_k", 1)], (17, 0): [("turn_gv", 0)],
           (18, 0): [("turn_gv", 1)], (19, 0): [("turn_gv", 2)], (20, 0): [("turn_gv", 3)],
           (20, 1): [("kv", 0)], (20, 2): [("kv", 1)], (21, 0): [("kv", 2)], (21, 1): [("o", 0)],
           (21, 2): [("kv", 3)], (22, 0): [("o", 1)], (22, 1): [("ms", 0), ("gated", 0)],
           (22, 2): [("ms", 1), ("gated", 1)], (23, 0): [("o", 2), ("o", 3)], (23, 1): [("ms", 2), ("ms", 3)],
           (23, 2): [("gated", 2), ("gated", 3)]}
    for t in range(9, 24):
        for part, (k0, k1) in enumerate(((0, 3), (3, 6), (6, KT))):
            order.append(("part", (t, k0, k1)))
            order += gla.get((t, part), [])
            if t < 22 and (t, part) not in ((9, 2), (10, 2), (11, 2), (20, 2), (21, 2)):
                attend()
    attend(N_ITEMS + 2 - step)
    return order


MIXER = mixer_schedule()
AUX2 = {e: n for n, e in enumerate(e for e in MIXER if e[0] in ("turn_v", "fg", "turn_k", "turn_gv", "kv", "o", "ms"))}


def item(m):
    h, i = m // 4, 3 - m % 4
    return h, i, P * i, S - P * i


def build(nc, a, out):
    ctx = ExitStack()
    with ctx:
        def sb(name, cols, dt=F32, parts=P):
            return ctx.enter_context(nc.sbuf_tensor(name, [parts, cols], dt))

        def sem(name):
            return ctx.enter_context(nc.semaphore(name))

        scratch = ExitStack()
        under_hi0 = scratch.enter_context(nc.sbuf_tensor("under_hi0", [P, KT * S], F32))
        under_lo0 = scratch.enter_context(nc.sbuf_tensor("under_lo0", [P, KT * S], F32))
        scratch.close()
        hi0 = sb("operand_hi0", KT * S, F32R)
        lo0 = sb("operand_lo0", KT * S, F32R)
        hi1 = sb("operand_hi1", KT * S, F32R)
        lo1 = sb("operand_lo1", KT * S, F32R)
        OP = [(hi0, lo0), (hi1, lo1)]
        raw = [sb(f"raw{j}", KT * UNIT) for j in range(2)]
        w_hi = [sb(f"weights_hi{k}", KT * P, F32R) for k in range(4)]
        w_lo = [sb(f"weights_lo{k}", KT * P, F32R) for k in range(4)]
        x = sb("x_features", KT * S)
        gates = sb("gates", KT * S)
        kept = sb("kept", KT * S)
        mixw = sb("mix_weights", 8 * P)
        mixb = sb("mix_bias", 8 * P)
        table = sb("vector_table", 512)
        mod = sb("modulation", NMOD * KT)
        scales = sb("mod_scales", 4 * KT)
        cvec = sb("c_silu", KT)
        ssum = sb("square_sums", S)
        spread = sb("inverse_rms_diagonals", S)
        rms = sb("rms_by_token", 2 * NBLK)
        tA = [sb(f"value{j}", S) for j in range(2)]
        tB = sb("evacuated", 2 * S)
        yb = sb("conv_or_gate", 4 * S)
        shared = sb("ada_or_attention", 6 * S)
        acc = sb("ada_sums", ADA)
        stat = sb("v_stats", 3 * NBLK)
        decay = sb("decay", 2 * NCH)
        raw_gf = sb("raw_gf", KT * RANK)
        ident = sb("identity", P)
        ones = sb("ones", P)
        columns2 = sb("mean_columns", 2)
        gain2 = sb("gain_of_two_norms", KT)
        mean_h = sb("mean_of_head", P)
        neg_one = sb("minus_ones", P)
        neg_tri = sb("minus_lower_triangle", P)
        before = sb("key_before_query", P)
        epsc = sb("eps", 1)

        ps = [ctx.enter_context(nc.psum_tensor(f"bank{k}", [P, S], F32)) for k in range(4)]
        aux = [ctx.enter_context(nc.psum_tensor(f"aux{k}", [P, S], F32)) for k in range(4)]

        gq = [mixw[:, p * S:(p + 1) * S] for p in range(2)]
        gk = [mixb[:, p * S:(p + 1) * S] for p in range(2)]
        gate_y = [under_hi0[:, (4 + p) * S:(5 + p) * S] for p in range(2)]
        gate_e = [under_hi0[:, (6 + p) * S:(7 + p) * S] for p in range(2)]
        states = under_hi0[:, 4 * S:8 * S]
        k_tok = under_lo0[:, 4 * S:6 * S]
        gf_t = under_lo0[0:RANK, 6 * S:7 * S]
        wfg = yb[0:RANK, 0:2 * P]
        E = [shared[:, j * S:(j + 1) * S] for j in range(3)]
        SP = [shared[:, (3 + j) * S:(4 + j) * S] for j in range(2)]
        later = shared[:, 5 * S:6 * S]
        ada_raw = shared[:, 0:KT * ADA]
        v_tok = kept[:, 0:4 * S]
        gv_tok = kept[:, 4 * S:8 * S]
        vec_rows = shared[:, 0:4 * P]
        ws_rows = kept[:, 1024:2048]

        ssum3 = yb[:, 2 * S:3 * S]
        one = ones[:, 0:1]
        sq3 = [yb[:, S:2 * S], yb[:, 3 * S:4 * S]]
        mean_w, eps_sq = (columns2[:, n:n + 1] for n in range(2))

        def tb(j):
            return tB[:, j * S:(j + 1) * S]

        X_BANKS = [aux[3], ps[3], ps[2], ps[1]]

        def tile(buf, n):
            return buf[:, bass.ds(n * S, S)]

        def col(c, n=1):
            return table[:, bass.ds(c, n)]

        vec_loaded, late_loaded, ws_loaded, small_loaded = (
            sem(n) for n in ("vec_loaded", "late_loaded", "ws_loaded", "small_loaded"))
        x_loaded = [sem(f"x_loaded{c}") for c in range(4)]
        consts, masks_begun = sem("consts"), sem("masks_begun")
        rows_turned, table_kept, ws_turned, ws_kept, x_turned, x_kept = (
            sem(n) for n in ("rows_turned", "table_kept", "ws_turned", "ws_kept", "x_turned", "x_kept"))
        c_ready, gain2_done = sem("c_ready"), sem("gain2_done")
        raw_landed = [sem(f"raw_landed{j}") for j in range(2)]
        w_hi_done, w_lo_done, tile_done = sem("w_hi_done"), sem("w_lo_done"), sem("tile_done")
        bank_read = [sem(f"bank_read{k}") for k in range(4)]
        value, act_hi, operand = sem("value"), sem("act_hi"), sem("operand")
        sq_done, sum_added, sq3_done, sum3_added, norm_summed, rms_done, inv_done, diag_done, norm_spread = (
            sem(n) for n in ("sq_done", "sum_added", "sq3_done", "sum3_added", "norm_summed", "rms_done", "inv_done",
                             "diag_done", "norm_spread"))
        v_turned, v_kept, v_sumsq, v_rms, v_inv, v_normed = (
            sem(n) for n in ("v_turned", "v_kept", "v_sumsq", "v_rms", "v_inv", "v_normed"))
        mixed, mix_biased, tap0, tap1, tap2 = (sem(n) for n in ("mixed", "mix_biased", "tap0", "tap1", "tap2"))
        ada_landed, ada_step, ada_turned, mod_done = (sem(n) for n in ("ada_landed", "ada_step", "ada_turned", "mod_done"))
        silu_done = sem("silu_done")
        aux2_filled, aux2_read = sem("aux2_filled"), sem("aux2_read")
        gf_hi, gf_lo = sem("gf_hi"), sem("gf_lo")
        g_abs, g_exp, g_log, g_sp, g_cum, g_rest, g_dec, k_dec, g_state, o_sq, g_inv, g_scaled = (
            sem(n) for n in ("g_abs", "g_exp", "g_log", "g_sp", "g_cum", "g_rest", "g_dec", "k_dec", "g_state",
                             "o_sq", "g_inv", "g_scaled"))
        reset_ready, gate_done = sem("reset_ready"), sem("gate_done")
        z_done, z_low, z_exp, z_log, sp_raw, sp_done, tri_done, w_exp, w_masked, pv_done, later_done = (
            sem(n) for n in ("z_done", "z_low", "z_exp", "z_log", "sp_raw", "sp_done", "tri_done", "w_exp",
                             "w_masked", "pv_done", "later_done"))
        attn_hi, attn_lo = sem("attn_hi"), sem("attn_lo")
        out_turned, out_kept, out_written = sem("out_turned"), sem("out_kept"), sem("out_written")

        block = ctx.enter_context(nc.Block())

        F = FIRST
        MIX_Q = F["w2"]
        LAST_K = (F2 - 2 * D) // P
        mixer_columns = [2 * S, 2 * S + UNIT, 0, UNIT, S, S + UNIT, 3 * S, 3 * S + UNIT,
                         4 * S, 4 * S + UNIT, 5 * S, 5 * S + UNIT]
        NORM = {name: n for n, name in enumerate(["n1", "n2", "n3", "between", "n4", "final"])}
        SUM = {name: n for n, name in enumerate(["n1", "n2", "between", "n4", "final"])}

        def rows(w):
            return w.rearrange("(k p) n -> p k n", p=P)

        @block.sync
        def _(sp):
            xt = a["x"][0].rearrange("(b p) n -> p b n", p=P)
            for c in range(4):
                cs = slice(c * 2 * P, (c + 1) * 2 * P)
                sp.dma_start(gates[:, :].rearrange("p (b n) -> p b n", b=NBLK)[:, :, cs], xt[:, :, cs])\
                  .then_inc(x_loaded[c], 16)

            def unit(q, j, w, row_tile, column, k_tiles=KT):
                if not (isinstance(q, int) and q == 0):
                    sp.wait_ge(w_lo_done, 4 * (q - 1) + 2 * j + 2)
                sp.dma_start(raw[j][:, 0:k_tiles * UNIT].rearrange("p (k n) -> p k n", n=UNIT),
                             rows(w)[:, bass.ds(row_tile, k_tiles), bass.ds(column, UNIT)])\
                  .then_inc(raw_landed[j], 16)

            def columns(q0, w, c0, n=2):
                with sp.Fori(0, n) as i:
                    for j in range(2):
                        unit(q0 + i, j, w, 0, c0 + 2 * UNIT * i + UNIT * j)

            w_in = a["w_in"][0]
            for j in range(2):
                unit(0, j, w_in, 0, D + UNIT * j)
            for j in range(2):
                unit(1, j, w_in, 0, D + 2 * UNIT + UNIT * j)
            columns(F["u"], w_in, 0)
            columns(F["ga"], w_in, 5 * D)
            columns(F["pa"], a["w_proj_a"][0], 0)
            columns(F["cg"], w_in, 3 * D)
            columns(F["xs"], w_in, 4 * D)
            columns(F["bg"], w_in, 2 * D)
            columns(F["gb"], w_in, 6 * D)
            columns(F["pb"], a["w_proj_b"][0], 0)
            columns(F["out"], a["w_out"][0], 0)
            with sp.Fori(0, 4) as c:
                for part in range(2):
                    with sp.Fori(0, 2) as i:
                        q = F["ff"] + 4 * c + 2 * part + i
                        for j in range(2):
                            if part == 0:
                                unit(q, j, a["w_ff1"][0], 0, D * c + 2 * UNIT * i + UNIT * j)
                            else:
                                unit(q, j, a["w_ff2"][0], KT * c, 2 * UNIT * i + UNIT * j)
            for u, c0 in enumerate(mixer_columns):
                unit(MIX_Q + u // 2, u % 2, a["w_in_2"][0], 0, c0)
            columns(F["out2"], a["w_out_2"][0], 0)
            w_up, w_down = a["w_up_2"][0], a["w_down_2"][0]
            with sp.Fori(0, 2) as c:
                with sp.Fori(0, 4) as i:
                    for j in range(2):
                        unit(F["mlp"] + 6 * c + i, j, w_up, 0, D * c + UNIT * i + F2 * j)
                with sp.Fori(0, 2) as i:
                    for j in range(2):
                        unit(F["mlp"] + 6 * c + 4 + i, j, w_down, KT * c, 2 * UNIT * i + UNIT * j)
            for i in range(3):
                for j in range(2):
                    unit(F["last_up"] + i, j, w_up, 0, 2 * D + UNIT * i + F2 * j)
            for i in range(2):
                for j in range(2):
                    unit(F["last_down"] + i, j, w_down, 2 * KT, 2 * UNIT * i + UNIT * j, LAST_K)

            ov = out[0].rearrange("(b p) n -> p b n", p=P)
            gv = gates[:, :].rearrange("p (b n) -> p b n", b=NBLK)
            for half in range(2):
                sp.wait_ge(out_kept, 4 * (half + 1))
                sp.dma_start(ov[:, :, half * S:(half + 1) * S], gv[:, :, half * S:(half + 1) * S])\
                  .then_inc(out_written, 16)
            sp.wait_ge(out_written, 32)

        @block.gpsimd
        def _(pool):
            pool.memset(ident[:, :], 0.0).then_inc(masks_begun, 1)
            pool.memset(neg_tri[:, :], -1.0).then_inc(masks_begun, 1)
            pool.memset(before[:, :], 1.0).then_inc(masks_begun, 1)
            pool.wait_ge(masks_begun, 3)
            pool.affine_select(out=ident[:, :], in_=ident[:, :], compare_op=ALU.not_equal, fill=1.0, base=0,
                               pattern=[[-1, P]], channel_multiplier=1).then_inc(consts, 1)
            pool.affine_select(out=neg_tri[:, :], in_=neg_tri[:, :], compare_op=ALU.is_ge, fill=0.0, base=0,
                               pattern=[[-1, P]], channel_multiplier=1).then_inc(consts, 1)
            pool.affine_select(out=before[:, :], in_=before[:, :], compare_op=ALU.is_gt, fill=0.0, base=0,
                               pattern=[[1, P]], channel_multiplier=-1).then_inc(consts, 1)
            pool.memset(ones[:, :], 1.0).then_inc(consts, 1)
            pool.memset(mean_w, 1.0 / D).then_inc(consts, 1)
            pool.memset(eps_sq, EPS * EPS).then_inc(consts, 1)
            pool.memset(mean_h[:, :], 1.0 / DV).then_inc(consts, 1)
            pool.memset(neg_one[:, :], -1.0).then_inc(consts, 1)
            pool.memset(epsc[:, :], EPS).then_inc(consts, 1)

            pool.dma_start(ws_rows.rearrange("p (g j) -> p g j", g=8),
                           a["w_s"][0].rearrange("g i j -> i g j")).then_inc(ws_loaded, 16)
            pool.dma_start(mixb[:, :], a["b_s"][0].rearrange("g i -> (g i)").partition_broadcast(P)).then_inc(small_loaded, 16)
            pool.dma_start(wfg, a["w_fg2_2"][0]).then_inc(small_loaded, 16)
            pool.dma_start(raw_gf[:, :].rearrange("p (k n) -> p k n", n=RANK),
                           rows(a["w_in_2"][0])[:, :, 6 * S:6 * S + RANK]).then_inc(small_loaded, 16)

            with pool.Fori(0, 16) as piece:
                pool.wait_ge(ada_step, 1 + KT * piece)
                pool.dma_start(ada_raw.rearrange("p (k n) -> p k n", n=ADA),
                               rows(a["w_ada_2"][0])[:, :, bass.ds(ADA * piece, ADA)]).then_inc(ada_landed, 16)

            for m in range(N_ITEMS):
                pool.wait_ge(w_exp, m + 1)
                e = E[m % 3][:, 0:P]
                pool.affine_select(out=e, in_=e, compare_op=ALU.is_gt, fill=0.0, base=0,
                                   pattern=[[1, P]], channel_multiplier=-1).then_inc(w_masked, 1)

        @block.tensor
        def _(pe):
            def stream(q, tiles, op, ready=None, k_tiles=KT, first=0, last=None):
                last = k_tiles if last is None else last
                if first == 0:
                    for k in tiles:
                        pe.wait_ge(w_lo_done, 4 * q + k + 1)
                        if not (isinstance(q, int) and q == 0):
                            pe.wait_ge(bank_read[k], q)
                a_hi, a_lo = OP[op]
                for kt in range(first, last):
                    if ready is not None:
                        ready(kt)
                    ah, al = a_hi[:, kt * S:(kt + 1) * S], a_lo[:, kt * S:(kt + 1) * S]
                    for k in tiles:
                        wh, wl = w_hi[k][:, kt * P:(kt + 1) * P], w_lo[k][:, kt * P:(kt + 1) * P]
                        pe.matmul(ps[k][:, :], wh, ah, start=(kt == 0), stop=False)
                        pe.matmul(ps[k][:, :], wh, al, start=False, stop=False)
                        mm = pe.matmul(ps[k][:, :], wl, ah, start=False, stop=(kt == k_tiles - 1))
                        if kt == k_tiles - 1:
                            mm.then_inc(tile_done, 1)

            def stream_quad(q, op, ready, k_tiles=KT):
                stream(q, (0, 1), op, ready, k_tiles)
                for k in (2, 3):
                    stream(q, (k,), op, None, k_tiles)

            def made(base):
                return lambda kt: pe.wait_ge(operand, base + kt + 1)

            def quads(name, op, base, n=2):
                with pe.Fori(0, n) as i:
                    stream_quad(F[name] + i, op, made(base))

            def turn(dst, src, signal):
                for b in range(NBLK):
                    mm = pe.transpose(dst[:, b * P:(b + 1) * P], src[:, b * P:(b + 1) * P], ident[:, :])
                mm.then_inc(signal, 1)

            def sum_squares(norm):
                if norm == "n3":
                    pe.wait_ge(sum3_added, 9)
                    sums = ssum3
                else:
                    pe.wait_ge(sum_added, 9 * SUM[norm] + 9)
                    sums = ssum[:, :]
                for b in range(NBLK):
                    mm = pe.matmul(aux[0][:, b:b + 1], sums[:, b * P:(b + 1) * P], mean_w, start=True, stop=True)
                mm.then_inc(norm_summed, 1)

            def spread_rms(norm, bank=1):
                pe.wait_ge(diag_done, NORM[norm] + 1)
                pe.matmul(aux[bank][:, :], ones[:, :], spread[:, :], start=True, stop=True).then_inc(norm_spread, 1)

            pe.wait_ge(consts, 9)
            for d in range(KT):
                if d % 2 == 0:
                    pe.wait_ge(x_loaded[d // 2], 16)
                if d >= 4:
                    pe.wait_ge(x_kept, d - 3)
                for b in range(NBLK):
                    mm = pe.transpose(X_BANKS[d % 4][:, b * P:(b + 1) * P],
                                      gates[:, b * D + d * P:b * D + (d + 1) * P], ident[:, :])
                mm.then_inc(x_turned, 1)
            pe.wait_ge(vec_loaded, 7 * 16)
            pe.transpose(aux[1][:, 0:80], vec_rows[0:80, 0:P], ident[0:80, 0:80]).then_inc(rows_turned, 1)
            pe.wait_ge(ws_loaded, 16)
            for g in range(8):
                bank = aux[2] if g < 4 else aux[3]
                if g == 4:
                    pe.wait_ge(x_kept, 5)
                mm = pe.transpose(bank[:, g % 4 * P:(g % 4 + 1) * P], ws_rows[:, g * P:(g + 1) * P], ident[:, :])
            mm.then_inc(ws_turned, 1)
            sum_squares("n1")
            spread_rms("n1")

            def v_turn(n):
                pe.wait_ge(bank_read[n % 4], n // 4 + 1)
                if n >= 2:
                    pe.wait_ge(v_kept, n - 1)
                turn(aux[n % 2], tb(n % 2), v_turned)

            def mix(g):
                if g == 0:
                    pe.wait_ge(ws_kept, 3)
                    pe.wait_ge(v_normed, NBLK)
                if g >= 2:
                    pe.wait_ge(mix_biased, g - 1)
                for b in range(NBLK):
                    mm = pe.matmul(aux[g % 2][:, b * P:(b + 1) * P], kept[:, b * D + g * P:b * D + (g + 1) * P],
                                   mixw[:, g * P:(g + 1) * P], start=True, stop=True)
                mm.then_inc(mixed, 1)

            stream(0, (0, 1), 0, made(MADE["n1"]))
            for n in range(2, 8):
                stream(n // 4, (n % 4,), 0)
                v_turn(n - 2)
            for n in range(8):
                stream(F["u"] + n // 4, (n % 4,), 0)
                if n == 0:
                    v_turn(6)
                    v_turn(7)
                if n >= 3:
                    mix(n - 3)
            for g in range(5, 8):
                mix(g)
            pe.wait_ge(late_loaded, 9 * 16)
            for g, n in ((1, 78), (2, P), (3, 3 * F2T - P + F2T)):
                mm = pe.transpose(aux[2][:, g * P:g * P + n], vec_rows[0:n, g * P:(g + 1) * P], ident[0:n, 0:n])
            mm.then_inc(rows_turned, 1)
            quads("ga", 0, MADE["n1"])
            quads("pa", 1, MADE["u"])
            quads("cg", 0, MADE["n1"])
            quads("xs", 0, MADE["n1"])
            quads("bg", 0, MADE["n1"])
            quads("gb", 0, MADE["n1"])
            quads("pb", 1, MADE["bg"])
            quads("out", 0, MADE["pb"])
            sum_squares("n2")
            spread_rms("n2")

            def ada_turn(piece):
                pe.wait_ge(ada_step, 1 + KT * piece)
                for m in range(3):
                    mm = pe.matmul(aux[3][:, bass.ds(3 * piece + m, 1)], acc[:, m * P:(m + 1) * P], one,
                                   start=True, stop=True)
                mm.then_inc(ada_turned, 1)

            with pe.Fori(0, 4) as c:
                for part in range(2):
                    with pe.Fori(0, 2) as i:
                        base = MADE["n2"] if part == 0 else MADE["ff"] + KT * c
                        q = F["ff"] + 4 * c + 2 * part + i
                        stream(q, (0, 1), 1 - part, made(base))
                        ada_turn(4 * c + 2 * part + i)
                        for k in (2, 3):
                            stream(q, (k,), 1 - part)
            ada_turn(16)
            sum_squares("n3")
            spread_rms("n3")

            def fill(event, work):
                if AUX2[event] > 0:
                    pe.wait_ge(aux2_read, AUX2[event])
                work().then_inc(aux2_filled, 1)

            def turn_into_aux2(src):
                for b in range(NBLK):
                    mm = pe.transpose(aux[2][:, b * P:(b + 1) * P], src[:, b * P:(b + 1) * P], ident[:, :])
                return mm

            def low_rank():
                pe.wait_ge(gf_lo, 1)
                for kt in range(KT):
                    wh, wl = hi0[:, kt * RANK:(kt + 1) * RANK], lo0[:, kt * RANK:(kt + 1) * RANK]
                    ah, al = hi1[:, kt * S:(kt + 1) * S], lo1[:, kt * S:(kt + 1) * S]
                    pe.matmul(aux[2][0:RANK, :], wh, ah, start=(kt == 0), stop=False)
                    pe.matmul(aux[2][0:RANK, :], wh, al, start=False, stop=False)
                    mm = pe.matmul(aux[2][0:RANK, :], wl, ah, start=False, stop=(kt == KT - 1))
                return mm

            def chunk_products(r):
                pair, par = r // 2, r % 2
                half = slice(par * CHUNK, (par + 1) * CHUNK)
                for b in range(NBLK):
                    for e in range(2):
                        h = 2 * pair + e
                        mm = pe.matmul(aux[2][e * DK:(e + 1) * DK, b * P:(b + 1) * P],
                                       k_tok[half, b * 2 * P + h * DK:b * 2 * P + (h + 1) * DK],
                                       gv_tok[half, b * S + h * DV:b * S + (h + 1) * DV], start=True, stop=True)
                return mm

            def read_states(h):
                part = slice(h % 2 * DK, (h % 2 + 1) * DK)
                for n in range(NCH):
                    st = (h // 2 * NCH + n) * DV
                    mm = pe.matmul(aux[2][:, n * CHUNK:(n + 1) * CHUNK], states[part, st:st + DV],
                                   gq[h // 2][part, n * CHUNK:(n + 1) * CHUNK], start=True, stop=True)
                return mm

            for event in MIXER:
                kind, n = event
                if kind == "tile":
                    if n == 0:
                        stream(MIX_Q, (0, 1), 1, made(MADE["n3"]))
                    elif n > 1:
                        stream(MIX_Q + n // 4, (n % 4,), 1)
                    if n == 1:
                        sum_squares("between")
                    if n == 2:
                        spread_rms("between", 3)
                elif kind == "part":
                    t, k0, k1 = n
                    stream(MIX_Q + t // 4, (t % 4,), 1, first=k0, last=k1)
                elif kind == "turn_v":
                    pe.wait_ge(bank_read[n], MIX_Q + 1)
                    fill(event, lambda: turn_into_aux2(tb(n % 2)))
                elif kind == "turn_gv":
                    pe.wait_ge(bank_read[n], MIX_Q + 5)
                    fill(event, lambda: turn_into_aux2(tb(n % 2)))
                elif kind == "fg" and n == 0:
                    fill(event, low_rank)
                elif kind == "fg":
                    if n == 1:
                        pe.wait_ge(small_loaded, 48)
                    fill(event, lambda: pe.matmul(aux[2][:, :], wfg[:, (n - 1) * P:n * P], gf_t, start=True, stop=True))
                elif kind == "turn_k":
                    pe.wait_ge(k_dec, n + 1)
                    fill(event, lambda: turn_into_aux2(gate_y[n]))
                elif kind == "kv":
                    fill(event, lambda: chunk_products(n))
                elif kind == "o":
                    pe.wait_ge(g_state, (NCH - 1) * (n // 2 + 1))
                    fill(event, lambda: read_states(n))
                elif kind == "ms":
                    pe.wait_ge(o_sq, n + 1)
                    fill(event, lambda: pe.matmul(aux[2][:, :], mean_h[:, :], tb(n % 2), start=True, stop=True))
                elif kind == "z":
                    h, i, t0, width = item(n)
                    part = slice(h % 2 * SB_DIM, (h % 2 + 1) * SB_DIM)
                    if i == 3:
                        pe.wait_ge(bank_read[h // 2], MIX_Q + 3)
                    if n >= 2:
                        pe.wait_ge(w_exp, n - 1)
                    q_t, k_t = tile(gates, h // 2), tile(gates, 4 + h // 2)
                    pe.matmul(aux[n % 2][:, 0:width], k_t[part, t0:t0 + P], q_t[part, t0:S],
                              start=True, stop=True).then_inc(z_done, 1)
                elif kind == "tri":
                    h, i, t0, width = item(n)
                    pe.wait_ge(sp_done, n + 1)
                    mm = pe.matmul(aux[n % 2][:, 0:width], neg_tri[:, :], SP[n % 2][:, 0:width],
                                   start=False, stop=True, skip_group_check=True)
                    if i < 3:
                        pe.wait_ge(later_done, 3 * h + 3 - i)
                        mm = pe.matmul(aux[n % 2][:, P:width], neg_one[:, :], later[:, t0 + P:S],
                                       start=False, stop=True, skip_group_check=True)
                    mm.then_inc(tri_done, 1)
                elif kind == "pv":
                    h, i, t0, width = item(n)
                    pe.wait_ge(w_masked, n + 1)
                    if n == 0:
                        pe.wait_ge(aux2_read, AUX2[("turn_v", 3)] + 1)
                        pe.wait_ge(x_kept, 2 * KT)
                    if i == 3 and h % 2 == 0 and h > 0:
                        pe.wait_ge(attn_lo, h // 2)
                    part = slice(h % 2 * SB_DIM, (h % 2 + 1) * SB_DIM)
                    pe.matmul(aux[3][part, t0:S], v_tok[:, i * S + h * SB_DIM:i * S + (h + 1) * SB_DIM],
                              E[n % 3][:, 0:width], start=(i == 3), stop=True,
                              skip_group_check=True).then_inc(pv_done, 1)

            def mixer_made(kt):
                if kt < 4:
                    pe.wait_ge(attn_lo, kt + 1)
                else:
                    pe.wait_ge(operand, MADE["gla"] + kt - 3)

            with pe.Fori(0, 2) as i:
                stream_quad(F["out2"] + i, 0, mixer_made)
            sum_squares("n4")
            spread_rms("n4")
            with pe.Fori(0, 2) as c:
                with pe.Fori(0, 4) as i:
                    stream_quad(F["mlp"] + 6 * c + i, 1, made(MADE["n4"]))
                with pe.Fori(0, 2) as i:
                    stream_quad(F["mlp"] + 6 * c + 4 + i, 0, made(MADE["mlp"] + KT * c))
            quads("last_up", 1, MADE["n4"], 3)
            with pe.Fori(0, 2) as i:
                stream_quad(F["last_down"] + i, 0, made(MADE["last"]), LAST_K)
            sum_squares("final")
            spread_rms("final")
            for n in range(KT):
                pe.wait_ge(value, VALUED["final"] + n + 1)
                if n >= 2:
                    pe.wait_ge(out_kept, n - 1)
                turn(aux[2 + n % 2], tA[n % 2], out_turned)

        @block.scalar
        def _(act):
            def weights(q, k, k_tiles=KT):
                if k % 2 == 0:
                    act.wait_ge(raw_landed[k // 2], 16 * (q + 1))
                if not (isinstance(q, int) and q == 0):
                    act.wait_ge(tile_done, 4 * (q - 1) + k + 1)
                src = raw[k // 2][:, 0:k_tiles * UNIT].rearrange("p (k n) -> p k n", n=UNIT)
                act.activation(w_hi[k][:, 0:k_tiles * P].rearrange("p (k n) -> p k n", n=P),
                               src[:, :, k % 2 * P:(k % 2 + 1) * P], ACT.Copy).then_inc(w_hi_done, 1)

            def round_operand(op, n, src, shift=None):
                if shift is None:
                    act.activation(tile(OP[op][0], n), src, ACT.Copy).then_inc(act_hi, 1)
                else:
                    act.activation(tile(OP[op][0], n), src, ACT.Identity, bias=shift).then_inc(act_hi, 1)

            def square(norm, n, slot):
                act.wait_ge(sum_added, 9 * SUM[norm] + max(n, 1))
                act.activation(tb(slot), tile(x, n), ACT.Square).then_inc(sq_done, 1)

            def norm(name, op, shift=None, meanwhile=None):
                act.preload_act_table(ACT.Sqrt)
                act.wait_ge(norm_summed, NORM[name] + 1)
                act.activation(rms[:, 0:NBLK], aux[0][:, 0:NBLK], ACT.Sqrt,
                               bias=eps_sq if name == "n3" else epsc[:, :]).then_inc(rms_done, 1)
                if meanwhile is not None:
                    meanwhile()
                if op is not None:
                    for n in range(KT):
                        act.wait_ge(value, VALUED[name] + n + 1)
                        round_operand(op, n, tA[n % 2][:, :], None if shift is None else mod[:, shift + n:shift + n + 1])

            vec = vec_rows.rearrange("p (g c) -> p g c", g=4)

            def load_rows(group, row, v, n):
                act.dma_start(vec[row:row + n, group, :], v.rearrange("(r c) -> r c", c=P))\
                   .then_inc(vec_loaded if group == 0 else late_loaded, 16)

            load_rows(0, 0, a["norm_mix_g"][0], 8)
            load_rows(0, 8, a["b_gate"][0], 16)
            load_rows(0, 24, a["norm_v_g"][0], 8)
            load_rows(0, 32, a["conv_w"][0].rearrange("k n -> (k n)"), 24)
            load_rows(0, 56, a["norm_ff_g"][0], 8)
            load_rows(0, 64, a["c_2"][0], 8)
            load_rows(0, 72, a["norm_final_g"], 8)

            act.wait_ge(consts, 9)
            for d in range(KT):
                act.wait_ge(x_kept, d + 1)
                square("n1", d, d % 2)
            for k in range(2):
                weights(0, k)
            norm("n1", 0, meanwhile=lambda: [weights(0, k) for k in (2, 3)])
            load_rows(1, 0, a["b_ada_2"][0], 48)
            load_rows(1, 48, a["g_norm1_2"][0], 8)
            load_rows(1, 56, a["b_fg2_2"][0], 2)
            load_rows(1, 58, a["g_gla_out_2"][0], 4)
            load_rows(1, 62, a["g_norm2_2"][0], 8)
            load_rows(1, 70, a["g_final_2"], 8)
            w_conv = a["w_conv_2"][0].rearrange("k n -> (k n)")
            load_rows(2, 0, w_conv[0:P * P], P)
            load_rows(3, 0, w_conv[P * P:], 3 * F2T - P)
            load_rows(3, 3 * F2T - P, a["b_conv_2"][0], F2T)
            act.activation(gain2[:, :], col(C_NFIN, KT), ACT.Square).then_inc(gain2_done, 1)
            act.wait_ge(gain2_done, 1)
            act.activation(gain2[:, :], gain2[:, :], ACT.Sqrt, bias=epsc[:, :]).then_inc(gain2_done, 1)
            act.activation(cvec[:, :], col(C_C, KT), ACT.Silu).then_inc(c_ready, 1)
            for n in range(8):
                q, k = n // 4, n % 4
                act.wait_ge(tile_done, n + 1)
                if n >= 2:
                    act.wait_ge(v_turned, n - 1)
                act.activation(tb(n % 2), ps[k][:, :], ACT.Gelu).then_inc(bank_read[k], 1)
                weights(q + 1, k)
            for n in range(8):
                q, k = F["u"] + n // 4, n % 4
                if n == 1:
                    act.wait_ge(v_kept, 8)
                    for b in range(NBLK):
                        if b > 0:
                            act.wait_ge(v_sumsq, b)
                        act.activation(tB[:, :], kept[:, b * D:(b + 1) * D], ACT.Square,
                                       accum_out=stat[:, b:b + 1]).then_inc(v_sumsq, 1)
                    act.wait_ge(v_sumsq, NBLK)
                    act.activation(stat[:, NBLK:2 * NBLK], stat[:, 0:NBLK], ACT.Sqrt, bias=epsc[:, :],
                                   scale=1.0 / D).then_inc(v_rms, 1)
                act.wait_ge(tile_done, 4 * q + k + 1)
                act.activation(tile(gates, n), ps[k][:, :], ACT.Gelu).then_inc(bank_read[k], 1)
                weights(q + 1, k)
                if n >= 3:
                    act.wait_ge(value, VALUED["u"] + n - 2)
                    round_operand(1, n - 3, tA[(n - 3) % 2][:, :])
            for n in range(5, 8):
                act.wait_ge(value, VALUED["u"] + n + 1)
                round_operand(1, n, tA[n % 2][:, :])

            def phase(name, work, n=2):
                with act.Fori(0, n) as i:
                    for k in range(4):
                        q = F[name] + i
                        act.wait_ge(tile_done, 4 * q + k + 1)
                        work(4 * i + k, q, k)
                        weights(q + 1, k)

            def sigmoid(c0):
                return lambda n, q, k: act.activation(tile(gates, n), ps[k][:, :], ACT.Sigmoid,
                                                      bias=col(c0 + n)).then_inc(bank_read[k], 1)

            def to_operand(op):
                def work(n, q, k):
                    act.wait_ge(bank_read[k], q + 1)
                    round_operand(op, n, tA[k % 2][:, :])
                return work

            def scale_last_tap(n, q, k):
                act.wait_ge(bank_read[k], q + 1)
                act.activation(tile(gates, n), tA[k % 2][:, :], ACT.Copy, scale=col(C_CONV + 2 * KT + n)).then_inc(tap0, 1)

            def projected(n, q, k):
                act.wait_ge(value, VALUED["pb"] + n + 1)
                round_operand(0, n, tA[k % 2][:, :])

            def square_x(name):
                def work(n, q, k):
                    act.wait_ge(bank_read[k], q + 1)
                    act.wait_ge(sum_added, 9 * SUM[name] + n)
                    act.activation(tb(k % 2), tile(x, n), ACT.Square).then_inc(sq_done, 1)
                return work

            nothing = lambda n, q, k: None
            phase("ga", sigmoid(C_BGATE))
            phase("pa", nothing)
            phase("cg", lambda n, q, k: act.activation(tile(gates, n), ps[k][:, :], ACT.Copy).then_inc(bank_read[k], 1))
            phase("xs", scale_last_tap)
            phase("bg", to_operand(1))
            phase("gb", sigmoid(C_BGATE + KT))
            phase("pb", projected)
            phase("out", square_x("n2"))
            norm("n2", 1)

            def ff_chunk(c, last):
                for part in range(2):
                    with act.Fori(0, 2) as i:
                        for k in range(4):
                            q = F["ff"] + 4 * c + 2 * part + i
                            act.wait_ge(tile_done, 4 * q + k + 1)
                            if part == 0:
                                n = KT * c + 4 * i + k
                                act.wait_ge(operand, MADE["ff"] + n - 1)
                                act.activation(tb(k % 2), ps[k][:, :], ACT.Relu).then_inc(bank_read[k], 1)
                                act.wait_ge(bank_read[k], q + 1)
                                act.activation(tA[k % 2][:, :], tb(k % 2), ACT.Square).then_inc(value, 1)
                                act.wait_ge(value, VALUED["ff"] + n + 1)
                                round_operand(0, 4 * i + k, tA[k % 2][:, :])
                            elif last:
                                square_x("between")(4 * i + k, q, k)
                                act.wait_ge(sum3_added, 4 * i + k)
                                act.activation(sq3[k % 2], tile(x, 4 * i + k), ACT.Square,
                                               scale=gain2[:, bass.ds(4 * i + k, 1)]).then_inc(sq3_done, 1)
                            weights(q + 1, k)

            act.wait_ge(gain2_done, 2)
            with act.Fori(0, 3) as c:
                ff_chunk(c, False)
            ff_chunk(3, True)
            act.wait_ge(small_loaded, 48)
            act.activation(hi0[:, 0:KT * RANK], raw_gf[:, :], ACT.Copy).then_inc(gf_hi, 1)
            norm("n3", 1, 0)

            for event in MIXER:
                kind, n = event
                if kind == "part":
                    if n[2] < KT:
                        continue
                    kind, n = "tile", n[0]
                if kind == "tile":
                    q, k = MIX_Q + n // 4, n % 4
                    if n == 2:
                        norm("between", None)
                        act.preload_act_table_set("natural_log_exp_and_others")
                    act.wait_ge(tile_done, 4 * q + k + 1)
                    if n < 4 or 16 <= n < 20:
                        if n < 4 and n >= 2:
                            act.wait_ge(aux2_filled, AUX2[("turn_v", n - 2)] + 1)
                        if n >= 18:
                            act.wait_ge(aux2_filled, AUX2[("turn_gv", n - 18)] + 1)
                        act.activation(tb(n % 2), ps[k][:, :], ACT.Copy).then_inc(bank_read[k], 1)
                    elif n < 8:
                        act.activation(tile(gates, n - 4), ps[k][:, :], ACT.Copy, scale=SB_DIM ** -0.5).then_inc(bank_read[k], 1)
                    elif n < 12:
                        act.activation(tile(gates, n - 4), ps[k][:, :], ACT.Copy).then_inc(bank_read[k], 1)
                    elif n < 14:
                        act.activation(gq[n - 12], ps[k][:, :], ACT.Copy, scale=DK ** -0.5).then_inc(bank_read[k], 1)
                    elif n < 16:
                        act.activation(gk[n - 14], ps[k][:, :], ACT.Copy).then_inc(bank_read[k], 1)
                    else:
                        act.activation(yb[:, (n - 20) * S:(n - 19) * S], ps[k][:, :], ACT.Copy).then_inc(bank_read[k], 1)
                    weights(q + 1, k)
                    if n in (21, 23):
                        for g in (n - 21, n - 20):
                            act.wait_ge(bank_read[g], MIX_Q + 6)
                        y = yb[:, (n - 21) * S:(n - 19) * S]
                        act.activation(y, y, ACT.Silu).then_inc(gate_done, 1)
                        if n == 21:
                            act.preload_act_table_set("natural_log_exp_and_others")
                elif kind == "fg" and n > 0:
                    p = n - 1
                    act.wait_ge(g_abs, p + 1)
                    act.activation(gate_e[p], gate_e[p], ACT.Exp, scale=-1.0).then_inc(g_exp, 1)
                    act.wait_ge(g_exp, p + 1)
                    act.activation(gate_e[p], gate_e[p], ACT.Ln, bias=one).then_inc(g_log, 1)
                    act.wait_ge(g_rest, p + 1)
                    act.activation(decay[:, p * NCH:(p + 1) * NCH], gate_e[p][:, CHUNK - 1:S:CHUNK], ACT.Exp,
                                   scale=-1.0 / TAU).then_inc(g_dec, 1)
                    act.activation(gate_y[p], gate_y[p], ACT.Exp, scale=-1.0 / TAU).then_inc(g_dec, 1)
                elif kind == "o":
                    act.wait_ge(aux2_filled, AUX2[event] + 1)
                    act.activation(tb(n % 2), aux[2][:, :], ACT.Square).then_inc(o_sq, 1)
                elif kind == "ms":
                    act.wait_ge(aux2_filled, AUX2[event] + 1)
                    act.activation(tb(n % 2), aux[2][:, :], ACT.Ln, bias=epsc[:, :]).then_inc(aux2_read, 1)
                    act.wait_ge(aux2_read, AUX2[event] + 1)
                    act.activation(tb(n % 2), tb(n % 2), ACT.Exp, scale=-0.5).then_inc(g_inv, 1)
                elif kind == "gated":
                    act.wait_ge(value, VALUED["gla"] + n + 1)
                    round_operand(0, 4 + n, tA[n % 2][:, :])
                elif kind == "z":
                    width = item(n)[3]
                    e = E[n % 3][:, 0:width]
                    act.wait_ge(z_low, n + 1)
                    act.activation(e, e, ACT.Exp).then_inc(z_exp, 1)
                    act.wait_ge(z_exp, n + 1)
                    act.activation(e, e, ACT.Ln, bias=one).then_inc(z_log, 1)
                elif kind == "tri":
                    width = item(n)[3]
                    act.wait_ge(tri_done, n + 1)
                    act.activation(E[n % 3][:, 0:width], aux[n % 2][:, 0:width], ACT.Exp).then_inc(w_exp, 1)
                elif kind == "pv" and n % 8 == 7:
                    act.wait_ge(pv_done, n + 1)
                    act.activation(tile(hi0, n // 8), aux[3][:, :], ACT.Copy).then_inc(attn_hi, 1)

            phase("out2", square_x("n4"))
            norm("n4", 1, 3 * KT)

            def up_tile(k, val):
                ct = val if k < 2 else F2T // 2 + val
                act.activation(yb[:, k * S:(k + 1) * S], ps[k][:, :], ACT.Identity, bias=col(C_BCONV + ct),
                               scale=col(C_WCONV + 2 * F2T + ct)).then_inc(tap0, 1)

            def up(q, i, c0, value_base, k_next=KT):
                for k in range(4):
                    act.wait_ge(tile_done, 4 * q + k + 1)
                    up_tile(k, c0 + k % 2)
                    weights(q + 1, k, k_next)
                    if k >= 2:
                        act.wait_ge(bank_read[k], q + 1)
                        act.activation(tb(k - 2), yb[:, k * S:(k + 1) * S], ACT.Silu).then_inc(silu_done, 1)
                        act.wait_ge(value, value_base + k - 1)
                        round_operand(0, 2 * i + k - 2, tA[k - 2][:, :])

            with act.Fori(0, 2) as c:
                with act.Fori(0, 4) as i:
                    up(F["mlp"] + 6 * c + i, i, KT * c + 2 * i, VALUED["mlp"] + KT * c + 2 * i)
                with act.Fori(0, 2) as i:
                    for k in range(4):
                        weights(F["mlp"] + 6 * c + 4 + i + 1, k)
            for i in range(3):
                up(F["last_up"] + i, i, 2 * KT + 2 * i, VALUED["last"] + 2 * i, LAST_K if i == 2 else KT)
            for i in range(2):
                for k in range(4):
                    square_x("final")(4 * i + k, F["last_down"] + i, k)
                    if i == 0:
                        weights(F["last_down"] + 1, k, LAST_K)
            norm("final", None)
            for n in range(KT):
                act.wait_ge(out_turned, n + 1)
                act.activation(gates[:, :].rearrange("p (b n) -> p b n", b=NBLK)[:, :, n * P:(n + 1) * P],
                               aux[2 + n % 2][:, :].rearrange("p (b n) -> p b n", b=NBLK), ACT.Copy).then_inc(out_kept, 1)

        @block.vector
        def _(dve):
            def weights(q, k, k_tiles=KT):
                dve.wait_ge(w_hi_done, 4 * q + k + 1)
                src = raw[k // 2][:, 0:k_tiles * UNIT].rearrange("p (k n) -> p k n", n=UNIT)
                dve.tensor_tensor(w_lo[k][:, 0:k_tiles * P].rearrange("p (k n) -> p k n", n=P),
                                  src[:, :, k % 2 * P:(k % 2 + 1) * P],
                                  w_hi[k][:, 0:k_tiles * P].bitcast(F32).rearrange("p (k n) -> p k n", n=P),
                                  ALU.subtract).then_inc(w_lo_done, 1)

            def rest(op, n, src, made_before, shift=None):
                dve.wait_ge(act_hi, made_before + 1)
                hi, lo = tile(OP[op][0], n).bitcast(F32), tile(OP[op][1], n)
                if shift is None:
                    dve.tensor_tensor(lo, src, hi, ALU.subtract).then_inc(operand, 1)
                else:
                    dve.scalar_tensor_tensor(out=lo, in0=src, scalar=shift, in1=hi, op0=ALU.add,
                                             op1=ALU.subtract).then_inc(operand, 1)
                dve.wait_ge(operand, made_before + 1)

            def clear_sum():
                dve.memset(ssum[:, :], 0.0).then_inc(sum_added, 1)

            def add_square(name, n, slot):
                count = SUM[name]
                dve.wait_ge(sq_done, 8 * count + n + 1)
                dve.wait_ge(sum_added, 9 * count + n + 1)
                dve.tensor_tensor(ssum[:, :], ssum[:, :], tb(slot), ALU.add).then_inc(sum_added, 1)

            def invert_rms(name):
                dve.wait_ge(rms_done, NORM[name] + 1)
                dve.reciprocal(rms[:, NBLK:2 * NBLK], rms[:, 0:NBLK]).then_inc(inv_done, 1)
                dve.wait_ge(inv_done, NORM[name] + 1)
                dve.tensor_tensor(spread[:, :].rearrange("p (b n) -> p b n", b=NBLK),
                                  ident[:, :].unsqueeze(1).to_broadcast([P, NBLK, P]),
                                  rms[:, NBLK:2 * NBLK].unsqueeze(2).to_broadcast([P, NBLK, P]),
                                  ALU.mult).then_inc(diag_done, 1)
                dve.wait_ge(norm_spread, NORM[name] + 1)

            def norm(name, op, gain, shift=None):
                invert_rms(name)

                def split(n):
                    rest(op, n, tA[n % 2][:, :], MADE[name] + n, None if shift is None else mod[:, shift + n:shift + n + 1])

                for n in range(KT):
                    if op is None and n >= 2:
                        dve.wait_ge(out_turned, n - 1)
                    dve.scalar_tensor_tensor(out=tA[n % 2][:, :], in0=tile(x, n), scalar=gain(n), in1=aux[1][:, :],
                                             op0=ALU.mult, op1=ALU.mult).then_inc(value, 1)
                    if op is not None and n >= 1:
                        split(n - 1)
                if op is not None:
                    split(KT - 1)

            clear_sum()
            for d in range(KT):
                dve.wait_ge(x_turned, d + 1)
                dve.tensor_copy(tile(x, d), X_BANKS[d % 4][:, :]).then_inc(x_kept, 1)
                if d >= 1:
                    add_square("n1", d - 1, (d - 1) % 2)
            add_square("n1", KT - 1, 1)
            dve.wait_ge(rows_turned, 1)
            dve.tensor_copy(table[:, 0:80], aux[1][:, 0:80]).then_inc(table_kept, 1)
            for k in range(2):
                weights(0, k)
            dve.wait_ge(table_kept, 1)
            norm("n1", 0, lambda n: col(C_NMIX + n))
            for k in (2, 3):
                weights(0, k)

            dve.wait_ge(ws_turned, 1)
            wv = mixw[:, :].rearrange("p (g i) -> p g i", g=8)
            for g in range(2):
                src = aux[2 + g][:, :].rearrange("p (g i) -> p g i", g=4)
                dve.tensor_copy(wv[:, 4 * g:4 * g + 4, :], src).then_inc(ws_kept, 1)
            dve.wait_ge(ws_kept, 2)
            dve.memset(wv[CHUNK:P, :, 0:CHUNK], 0.0).then_inc(ws_kept, 1)

            def keep_v(n):
                dve.wait_ge(v_turned, n + 1)
                dve.tensor_copy(kept[:, :].rearrange("p (b n) -> p b n", b=NBLK)[:, :, n * P:(n + 1) * P],
                                aux[n % 2][:, :].rearrange("p (b n) -> p b n", b=NBLK)).then_inc(v_kept, 1)

            def mixed_value(g):
                if g == 0:
                    dve.wait_ge(small_loaded, 48)
                dve.wait_ge(mixed, g + 1)
                bias = mixb[:, g * P:(g + 1) * P].unsqueeze(1).to_broadcast([P, NBLK, P])
                dve.scalar_tensor_tensor(out=tA[g % 2][:, :].rearrange("p (b n) -> p b n", b=NBLK),
                                         in0=aux[g % 2][:, :].rearrange("p (b n) -> p b n", b=NBLK),
                                         scalar=col(C_NV + g), in1=bias, op0=ALU.mult, op1=ALU.add).then_inc(mix_biased, 1)
                dve.wait_ge(mix_biased, g + 1)
                dve.wait_ge(bank_read[g % 4], F["u"] + g // 4 + 1)
                dve.tensor_tensor(tA[g % 2][:, :], tA[g % 2][:, :], tile(gates, g), ALU.mult).then_inc(value, 1)
                rest(1, g, tA[g % 2][:, :], MADE["u"] + g)

            for n in range(8):
                if n >= 1:
                    weights((n - 1) // 4 + 1, (n - 1) % 4)
                if n >= 1:
                    keep_v(n - 1)
            weights(2, 3)
            for n in range(8):
                q, k = F["u"] + n // 4, n % 4
                if n == 0:
                    keep_v(7)
                if n == 1:
                    dve.wait_ge(v_rms, 1)
                    dve.reciprocal(stat[:, 2 * NBLK:3 * NBLK], stat[:, NBLK:2 * NBLK]).then_inc(v_inv, 1)
                    dve.wait_ge(v_inv, 1)
                    for b in range(NBLK):
                        dve.tensor_scalar(kept[:, b * D:(b + 1) * D], kept[:, b * D:(b + 1) * D],
                                          stat[:, 2 * NBLK + b:2 * NBLK + b + 1], None, ALU.mult).then_inc(v_normed, 1)
                weights(q + 1, k)
                if n >= 3:
                    mixed_value(n - 3)
            for g in range(5, 8):
                mixed_value(g)
            dve.wait_ge(rows_turned, 2)
            dve.tensor_copy(table[:, 128:206], aux[2][:, 128:206])
            dve.tensor_copy(table[:, 256:432], aux[2][:, 256:432]).then_inc(table_kept, 1)
            dve.wait_ge(table_kept, 2)
            dve.memset(acc[:, :], 0.0).then_inc(ada_step, 1)

            def phase(name, work, after=None, n=2):
                with dve.Fori(0, n) as i:
                    for k in range(4):
                        q = F[name] + i
                        if work is not None:
                            dve.wait_ge(tile_done, 4 * q + k + 1)
                            work(4 * i + k, q, k)
                        if after is not None:
                            after(4 * i + k, q, k)
                        weights(q + 1, k)

            def product(dst, src):
                def work(n, q, k):
                    dve.tensor_tensor(dst(n, k), ps[k][:, :], src(n), ALU.mult).then_inc(bank_read[k], 1)
                return work

            def to_value(n, k):
                return tA[k % 2][:, :]

            def taps(n, q, k):
                z, y = tA[k % 2], gates
                for j, (ready, signal) in enumerate(((tap0, tap1), (tap1, tap2))):
                    dve.wait_ge(ready, n + 1)
                    d = j + 1
                    yv = y[:, bass.ds(n * S + d, S - d)]
                    dve.scalar_tensor_tensor(out=yv, in0=z[:, 0:S - d], scalar=col(C_CONV + (1 - j) * KT + n), in1=yv,
                                             op0=ALU.mult, op1=ALU.add).then_inc(signal, 1)
                dve.wait_ge(tap2, n + 1)

            def gate_conv(n, q, k):
                dve.wait_ge(tap2, n + 1)
                product(to_value, lambda m: tile(gates, m))(n, q, k)

            def add_kept(n, q, k):
                dve.wait_ge(bank_read[k], q + 1)
                dve.tensor_tensor(tA[k % 2][:, :], tA[k % 2][:, :], tile(kept, n), ALU.add).then_inc(value, 1)
                rest(0, n, tA[k % 2][:, :], MADE["pb"] + n)

            def grow_x(n, q, k):
                dve.tensor_tensor(tile(x, n), tile(x, n), ps[k][:, :], ALU.add).then_inc(bank_read[k], 1)

            phase("ga", None)
            phase("pa", product(lambda n, k: tile(kept, n), lambda n: tile(gates, n)))
            phase("cg", None)
            phase("xs", product(to_value, lambda n: tile(gates, n)), taps)
            phase("bg", gate_conv, lambda n, q, k: rest(1, n, tA[k % 2][:, :], MADE["bg"] + n))
            phase("gb", None)
            phase("pb", product(to_value, lambda n: tile(gates, n)), add_kept)
            clear_sum()
            phase("out", grow_x, lambda n, q, k: add_square("n2", n, k % 2))
            norm("n2", 1, lambda n: col(C_NFF + n))

            def ff_chunk(c, last):
                if last:
                    clear_sum()
                    dve.memset(ssum3, 0.0).then_inc(sum3_added, 1)
                for part in range(2):
                    with dve.Fori(0, 2) as i:
                        for k in range(4):
                            q = F["ff"] + 4 * c + 2 * part + i
                            n = 4 * i + k
                            piece = 4 * c + 2 * part + i
                            if part == 1:
                                dve.wait_ge(tile_done, 4 * q + k + 1)
                            if part == 0:
                                rest(0, n, tA[k % 2][:, :], MADE["ff"] + KT * c + n)
                            else:
                                grow_x(n, q, k)
                            if not last or part == 0:
                                weights(q + 1, k)
                            if k == 1:
                                dve.wait_ge(ada_landed, 16 * (piece + 1))
                                dve.wait_ge(ada_turned, piece + 1)
                            if k in (1, 2):
                                for kt in range(4 * (k - 1), 4 * k):
                                    src = ada_raw[:, kt * ADA:(kt + 1) * ADA]
                                    if kt == 0:
                                        dve.tensor_scalar(acc[:, :], src, cvec[:, kt:kt + 1], None, ALU.mult)\
                                           .then_inc(ada_step, 1)
                                    else:
                                        dve.wait_ge(ada_step, 1 + KT * piece + kt)
                                        dve.scalar_tensor_tensor(out=acc[:, :], in0=src, scalar=cvec[:, kt:kt + 1],
                                                                 in1=acc[:, :], op0=ALU.mult, op1=ALU.add)\
                                           .then_inc(ada_step, 1)
                            if last and part == 1:
                                add_square("between", n, k % 2)
                                dve.wait_ge(sq3_done, n + 1)
                                dve.wait_ge(sum3_added, n + 1)
                                dve.tensor_tensor(ssum3, ssum3, sq3[k % 2], ALU.add).then_inc(sum3_added, 1)
                                weights(q + 1, k)

            dve.wait_ge(c_ready, 1)
            with dve.Fori(0, 3) as c:
                ff_chunk(c, False)
            ff_chunk(3, True)

            dve.wait_ge(ada_turned, 17)
            dve.tensor_tensor(mod[:, :], aux[3][:, 3:3 + NMOD * KT], col(C_BADA, NMOD * KT), ALU.add).then_inc(mod_done, 1)
            dve.wait_ge(mod_done, 1)
            for s, m, g in ((0, 1, C_G1), (1, 4, C_G2)):
                dve.scalar_tensor_tensor(out=scales[:, s * KT:(s + 1) * KT], in0=mod[:, m * KT:(m + 1) * KT], scalar=1.0,
                                         in1=col(g, KT), op0=ALU.add, op1=ALU.mult).then_inc(mod_done, 1)
            for s, m in ((2, 2), (3, 5)):
                dve.tensor_scalar(scales[:, s * KT:(s + 1) * KT], mod[:, m * KT:(m + 1) * KT], 1.0, None,
                                  ALU.add).then_inc(mod_done, 1)
            dve.wait_ge(gf_hi, 1)
            dve.tensor_tensor(lo0[:, 0:KT * RANK], raw_gf[:, :], hi0[:, 0:KT * RANK].bitcast(F32),
                              ALU.subtract).then_inc(gf_lo, 1)
            dve.wait_ge(mod_done, 5)
            dve.tensor_tensor(scales[:, 0:KT], scales[:, 0:KT], col(C_NFIN, KT), ALU.mult).then_inc(mod_done, 1)
            dve.wait_ge(mod_done, 6)
            norm("n3", 1, lambda n: scales[:, n:n + 1], 0)
            def keep_turned(event, dst):
                dve.wait_ge(aux2_filled, AUX2[event] + 1)
                dve.tensor_copy(dst, aux[2][:, :].rearrange("p (b n) -> p b n", b=NBLK)).then_inc(aux2_read, 1)

            def softplus_gate(p, event):
                y, e = gate_y[p], gate_e[p]
                dve.wait_ge(aux2_filled, AUX2[event] + 1)
                dve.tensor_scalar(y, aux[2][:, :], col(C_BFG + p), -1.0, ALU.add, ALU.mult).then_inc(aux2_read, 1)
                dve.wait_ge(aux2_read, AUX2[event] + 1)
                dve.scalar_tensor_tensor(out=e, in0=y, scalar=-1.0, in1=y, op0=ALU.mult, op1=ALU.max).then_inc(g_abs, 1)
                dve.wait_ge(g_log, p + 1)
                dve.scalar_tensor_tensor(out=y, in0=y, scalar=0.0, in1=e, op0=ALU.max, op1=ALU.add).then_inc(g_sp, 1)
                dve.wait_ge(g_sp, p + 1)
                dve.wait_ge(reset_ready, 2)
                dve.tensor_tensor_scan(e, spread[:, :], y, 0.0, ALU.mult, ALU.add).then_inc(g_cum, 1)
                dve.wait_ge(g_cum, p + 1)
                ev = e.rearrange("p (c s) -> p c s", s=CHUNK)
                dve.tensor_tensor(y.rearrange("p (c s) -> p c s", s=CHUNK),
                                  ev[:, :, CHUNK - 1:CHUNK].to_broadcast([P, NCH, CHUNK]), ev,
                                  ALU.subtract).then_inc(g_rest, 1)

            for event in MIXER:
                kind, n = event
                if kind == "part":
                    if n[2] < KT:
                        continue
                    kind, n = "tile", n[0]
                if kind == "tile":
                    weights(MIX_Q + n // 4 + 1, n % 4)
                    if n == 1:
                        invert_rms("between")
                    if 2 <= n < 6:
                        for d in range(2 * n - 4, 2 * n - 2):
                            dve.scalar_tensor_tensor(out=tile(x, d), in0=tile(x, d), scalar=col(C_NFIN + d),
                                                     in1=aux[3][:, :], op0=ALU.mult, op1=ALU.mult).then_inc(x_kept, 1)
                    if n == 6:
                        dve.memset(spread[:, :], 1.0).then_inc(reset_ready, 1)
                        dve.wait_ge(reset_ready, 1)
                        dve.memset(spread[:, 0:S:CHUNK], 0.0).then_inc(reset_ready, 1)
                elif kind == "turn_v":
                    keep_turned(event, v_tok.rearrange("p (b n) -> p b n", b=NBLK)[:, :, n * P:(n + 1) * P])
                elif kind == "turn_gv":
                    keep_turned(event, gv_tok.rearrange("p (b n) -> p b n", b=NBLK)[:, :, n * P:(n + 1) * P])
                elif kind == "turn_k":
                    dve.wait_ge(g_dec, 2 * n + 2)
                    dve.wait_ge(bank_read[2 + n], MIX_Q + 4)
                    dve.tensor_tensor(gate_y[n], gk[n], gate_y[n], ALU.mult).then_inc(k_dec, 1)
                    keep_turned(event, k_tok.rearrange("p (b n) -> p b n", b=NBLK)[:, :, n * P:(n + 1) * P])
                elif kind == "fg" and n == 0:
                    dve.wait_ge(aux2_filled, AUX2[event] + 1)
                    dve.tensor_copy(gf_t, aux[2][0:RANK, :]).then_inc(aux2_read, 1)
                elif kind == "fg":
                    softplus_gate(n - 1, event)
                elif kind == "kv":
                    pair, par = n // 2, n % 2
                    dve.wait_ge(aux2_filled, AUX2[event] + 1)
                    dst = states[:, pair * NCH * DV:(pair + 1) * NCH * DV].rearrange("p (b c n) -> p b c n", c=2, n=DV)
                    dve.tensor_copy(dst[:, :, par, :], aux[2][:, :].rearrange("p (b n) -> p b n", b=NBLK)).then_inc(aux2_read, 1)
                    if par == 1:
                        dve.wait_ge(aux2_read, AUX2[event] + 1)
                        for c in range(1, NCH):
                            st = (pair * NCH + c) * DV
                            if c > 1:
                                dve.wait_ge(g_state, (NCH - 1) * pair + c - 1)
                            dve.scalar_tensor_tensor(out=states[:, st:st + DV], in0=states[:, st - DV:st],
                                                     scalar=decay[:, pair * NCH + c:pair * NCH + c + 1],
                                                     in1=states[:, st:st + DV], op0=ALU.mult, op1=ALU.add).then_inc(g_state, 1)
                elif kind == "o":
                    dve.wait_ge(o_sq, n + 1)
                    dve.tensor_scalar(tA[n % 2][:, :], aux[2][:, :], col(C_GGLA + n), None, ALU.mult).then_inc(aux2_read, 1)
                elif kind == "ms":
                    dve.wait_ge(g_inv, n + 1)
                    dve.tensor_tensor(tA[n % 2][:, :], tA[n % 2][:, :], tb(n % 2), ALU.mult).then_inc(g_scaled, 1)
                elif kind == "gated":
                    dve.wait_ge(g_scaled, n + 1)
                    dve.wait_ge(gate_done, n // 2 + 1)
                    dve.tensor_tensor(tA[n % 2][:, :], tA[n % 2][:, :], yb[:, n * S:(n + 1) * S], ALU.mult).then_inc(value, 1)
                    rest(0, 4 + n, tA[n % 2][:, :], MADE["gla"] + n)
                elif kind == "z":
                    h, i, t0, width = item(n)
                    e, zb = E[n % 3][:, 0:width], aux[n % 2][:, 0:width]
                    dve.wait_ge(z_done, n + 1)
                    if n >= 3:
                        dve.wait_ge(pv_done, n - 2)
                    dve.tensor_scalar(e, zb, Z_BOUND, None, ALU.min).then_inc(z_low, 1)
                    dve.wait_ge(z_log, n + 1)
                    if n >= 2:
                        dve.wait_ge(tri_done, n - 1)
                    dve.tensor_tensor(SP[n % 2][:, 0:width], zb, e, ALU.max).then_inc(sp_raw, 1)
                    dve.wait_ge(sp_raw, n + 1)
                    dve.tensor_tensor(SP[n % 2][:, 0:P], SP[n % 2][:, 0:P], before[:, :], ALU.mult).then_inc(sp_done, 1)
                elif kind == "tri":
                    h, i, t0, width = item(n)
                    if i > 0:
                        dve.wait_ge(tri_done, n + 1)
                        new = dve.tensor_copy(later[:, t0:t0 + P], SP[n % 2][:, 0:P])
                        if i < 3:
                            dve.tensor_tensor(later[:, t0 + P:S], later[:, t0 + P:S], SP[n % 2][:, P:width],
                                              ALU.add).then_inc(later_done, 1)
                        else:
                            new.then_inc(later_done, 1)
                        dve.wait_ge(later_done, 3 * h + 4 - i)
                elif kind == "pv" and n % 8 == 7:
                    dve.wait_ge(attn_hi, n // 8 + 1)
                    dve.tensor_tensor(tile(lo0, n // 8), aux[3][:, :], tile(hi0, n // 8).bitcast(F32),
                                      ALU.subtract).then_inc(attn_lo, 1)

            clear_sum()

            def grow_scaled(s):
                def work(n, q, k):
                    dve.scalar_tensor_tensor(out=tile(x, n), in0=ps[k][:, :], scalar=scales[:, bass.ds(s * KT + n, 1)],
                                             in1=tile(x, n), op0=ALU.mult, op1=ALU.add).then_inc(bank_read[k], 1)
                return work

            phase("out2", grow_scaled(2), lambda n, q, k: add_square("n4", n, k % 2))
            norm("n4", 1, lambda n: scales[:, KT + n:KT + n + 1], 3 * KT)

            def up(q, i, c0, done, made_base, k_next=KT):
                for k in range(4):
                    ct = c0 + k % 2 + (F2T // 2 if k >= 2 else 0)
                    y = yb[:, k * S:(k + 1) * S]
                    dve.wait_ge(tap0, KT + 4 * done + k + 1)
                    dve.scalar_tensor_tensor(out=y[:, 1:S], in0=ps[k][:, 0:S - 1], scalar=col(C_WCONV + F2T + ct),
                                             in1=y[:, 1:S], op0=ALU.mult, op1=ALU.add).then_inc(tap1, 1)
                    dve.wait_ge(tap1, KT + 4 * done + k + 1)
                    dve.scalar_tensor_tensor(out=y[:, 2:S], in0=ps[k][:, 0:S - 2], scalar=col(C_WCONV + ct),
                                             in1=y[:, 2:S], op0=ALU.mult, op1=ALU.add).then_inc(bank_read[k], 1)
                    weights(q + 1, k, k_next)
                    if k >= 2:
                        dve.wait_ge(silu_done, 2 * done + k - 1)
                        dve.wait_ge(bank_read[k - 2], q + 1)
                        dve.tensor_tensor(tA[k - 2][:, :], yb[:, (k - 2) * S:(k - 1) * S], tb(k - 2),
                                          ALU.mult).then_inc(value, 1)
                        rest(0, 2 * i + k - 2, tA[k - 2][:, :], made_base + 2 * i + k - 2)

            with dve.Fori(0, 2) as c:
                with dve.Fori(0, 4) as i:
                    up(F["mlp"] + 6 * c + i, i, KT * c + 2 * i, 4 * c + i, MADE["mlp"] + KT * c)
                with dve.Fori(0, 2) as i:
                    for k in range(4):
                        q = F["mlp"] + 6 * c + 4 + i
                        dve.wait_ge(tile_done, 4 * q + k + 1)
                        grow_scaled(3)(4 * i + k, q, k)
                        weights(q + 1, k)
            for i in range(3):
                up(F["last_up"] + i, i, 2 * KT + 2 * i, 8 + i, MADE["last"], LAST_K if i == 2 else KT)
            clear_sum()
            for i in range(2):
                for k in range(4):
                    q = F["last_down"] + i
                    dve.wait_ge(tile_done, 4 * q + k + 1)
                    grow_scaled(3)(4 * i + k, q, k)
                    add_square("final", 4 * i + k, k % 2)
                    if i == 0:
                        weights(q + 1, k, LAST_K)
            norm("final", None, lambda n: col(C_GFIN + n))


INPUTS = ["x", "norm_mix_g", "w_in", "b_gate", "norm_v_g", "w_s", "b_s", "conv_w", "w_proj_a", "w_proj_b", "w_out",
          "norm_ff_g", "w_ff1", "w_ff2", "norm_final_g", "c_2", "w_ada_2", "b_ada_2", "g_norm1_2", "w_in_2", "w_fg2_2", "b_fg2_2",
          "g_gla_out_2", "w_out_2", "g_norm2_2", "w_up_2", "w_conv_2", "b_conv_2", "w_down_2", "g_final_2"]


def kernel(**inputs):
    import numpy as np
    from concourse import bacc
    from concourse.bass_utils import run_bass_kernel_spmd

    nc = bacc.Bacc("TRN2", target_bir_lowering=False, num_devices=1)
    arrays, aps = {}, {}
    for name in INPUTS:
        array = np.ascontiguousarray(inputs[name])
        arrays[f"in_{name}"] = array
        aps[name] = nc.dram_tensor(f"in_{name}", array.shape, mybir.dt.from_np(array.dtype), kind="ExternalInput").ap()
    out = nc.dram_tensor("out", (1, S, D), F32, kind="ExternalOutput").ap()
    build(nc, aps, out)
    result = run_bass_kernel_spmd(nc, [arrays], core_ids=[0])
    return result.results[0]["out"]
```
